# Optimizing a Trainium2 kernel written in Bass

```python
import jax, jax.numpy as jnp
from jax import lax
import numpy as np

D_MODEL = 1024
BATCH = 1
SEQ = 1024
DEPTH = 2

CHUNK = 64
N_MIXERS = 3
HEAD_DIM = 64
ROPE_THETA = 10000.0
NORM_EPS = 1e-6
SWA_HEADS = D_MODEL // HEAD_DIM
SWA_KV_HEADS = SWA_HEADS // 8
SWA_GROUP = SWA_HEADS // SWA_KV_HEADS
SWA_WINDOW = 128
SWA_WINDOW_CHUNKS = SWA_WINDOW // CHUNK
SWA_KEYS = SWA_WINDOW_CHUNKS * CHUNK
SWA_Q_WIDTH = SWA_HEADS * HEAD_DIM
SWA_KV_WIDTH = SWA_KV_HEADS * HEAD_DIM
GMLP_BLOCK = 128
GMLP_WIDTH = 2 * D_MODEL
GMLP_GROUPS = 8
GMLP_GROUP_WIDTH = GMLP_WIDTH // GMLP_GROUPS
SB_HEADS = D_MODEL // HEAD_DIM
SB_BLOCK = 128
MLP_HIDDEN = 4 * D_MODEL
N_SWA_LAYERS = (DEPTH + N_MIXERS - 1) // N_MIXERS
N_GMLP_LAYERS = (DEPTH + N_MIXERS - 2) // N_MIXERS
N_SB_LAYERS = (DEPTH + N_MIXERS - 3) // N_MIXERS
MAX_POS_OFFSET = 4096

kernel_name = 'hybrid_chunk_causal_swa_gmlp_stickbreaking_trunk'

def rms_norm(x, gain):
    xf = x.astype(jnp.float32)
    y = xf * lax.rsqrt(jnp.mean(xf * xf, axis=-1, keepdims=True) + NORM_EPS)
    return (y * gain.astype(jnp.float32)).astype(x.dtype)

def layer_norm(x, gain):
    xf = x.astype(jnp.float32)
    mu = jnp.mean(xf, axis=-1, keepdims=True)
    var = jnp.mean(jnp.square(xf - mu), axis=-1, keepdims=True)
    return ((xf - mu) * lax.rsqrt(var + NORM_EPS) * gain.astype(jnp.float32)).astype(x.dtype)

def rope(x, positions):
    d = x.shape[-1]
    inv_freq = ROPE_THETA ** (-jnp.arange(0, d, 2, dtype=jnp.float32) / d)
    ang = positions.astype(jnp.float32)[..., None] * inv_freq
    cos = jnp.cos(ang)[:, :, None, :]
    sin = jnp.sin(ang)[:, :, None, :]
    xf = x.astype(jnp.float32)
    x1, x2 = jnp.split(xf, 2, axis=-1)
    out = jnp.concatenate([x1 * cos - x2 * sin, x2 * cos + x1 * sin], axis=-1)
    return out.astype(x.dtype)

def swa_sink_attention(h, positions, w_qkv, q_gain, k_gain, sinks, w_o):
    B, S, _ = h.shape
    n_chunks = S // CHUNK
    q, k, v = jnp.split(h @ w_qkv, [SWA_Q_WIDTH, SWA_Q_WIDTH + SWA_KV_WIDTH], axis=-1)
    q = q.reshape(B, S, SWA_HEADS, HEAD_DIM)
    k = k.reshape(B, S, SWA_KV_HEADS, HEAD_DIM)
    v = v.reshape(B, S, SWA_KV_HEADS, HEAD_DIM)
    q = rope(rms_norm(q, q_gain), positions)
    k = rope(rms_norm(k, k_gain), positions)
    q = q.reshape(B, n_chunks, CHUNK, SWA_KV_HEADS, SWA_GROUP, HEAD_DIM)
    k = k.reshape(B, n_chunks, CHUNK, SWA_KV_HEADS, HEAD_DIM)
    v = v.reshape(B, n_chunks, CHUNK, SWA_KV_HEADS, HEAD_DIM)

    def shift(t, lag):
        if lag == 0:
            return t
        return jnp.pad(t, ((0, 0), (lag, 0), (0, 0), (0, 0), (0, 0)))[:, :n_chunks]

    lags = range(SWA_WINDOW_CHUNKS - 1, -1, -1)
    kk = jnp.concatenate([shift(k, j) for j in lags], axis=2)
    vv = jnp.concatenate([shift(v, j) for j in lags], axis=2)
    key_lag = (SWA_WINDOW_CHUNKS - 1) - jnp.arange(SWA_KEYS) // CHUNK
    valid = (jnp.arange(n_chunks)[:, None] - key_lag[None, :]) >= 0

    scores = jnp.einsum('bnqhgd,bnkhd->bnhgqk', q, kk).astype(jnp.float32) * (HEAD_DIM ** -0.5)
    scores = jnp.where(valid[None, :, None, None, None, :], scores, -jnp.inf)
    sink = sinks.astype(jnp.float32).reshape(SWA_KV_HEADS, SWA_GROUP)[None, None, :, :, None, None]
    m = jnp.maximum(jnp.max(scores, axis=-1, keepdims=True), sink)
    p = jnp.exp(scores - m)
    probs = p / (jnp.sum(p, axis=-1, keepdims=True) + jnp.exp(sink - m))
    o = jnp.einsum('bnhgqk,bnkhd->bnqhgd', probs.astype(vv.dtype), vv)
    return o.reshape(B, S, SWA_Q_WIDTH) @ w_o

def gmlp_spatial_gating(h, w_uv, v_gain, w_s, s_bias, w_o):
    B, S, _ = h.shape
    n_blocks = S // GMLP_BLOCK
    uv = jax.nn.gelu(h @ w_uv, approximate=False)
    u, v = jnp.split(uv, 2, axis=-1)
    v = layer_norm(v, v_gain)
    v = v.reshape(B, n_blocks, GMLP_BLOCK, GMLP_GROUPS, GMLP_GROUP_WIDTH)
    chunk_of = jnp.arange(GMLP_BLOCK) // CHUNK
    mask = chunk_of[None, :] <= chunk_of[:, None]
    w = jnp.where(mask[None], w_s, 0).astype(v.dtype)
    s = jnp.einsum('gij,bnjgc->bnigc', w, v) + s_bias.T[None, None, :, :, None].astype(v.dtype)
    return (u * s.reshape(B, S, GMLP_WIDTH)) @ w_o

def stick_breaking_attention(h, w_qkv, w_o):
    B, S, _ = h.shape
    q, k, v = jnp.split(h @ w_qkv, 3, axis=-1)
    q = q.reshape(B, S, SB_HEADS, HEAD_DIM)
    k = k.reshape(B, S, SB_HEADS, HEAD_DIM)
    v = v.reshape(B, S, SB_HEADS, HEAD_DIM)
    outs = []
    for n in range(S // SB_BLOCK):
        q0 = n * SB_BLOCK
        kl = q0 + SB_BLOCK
        z = jnp.einsum('bqhd,bkhd->bhqk', q[:, q0:kl], k[:, :kl]).astype(jnp.float32) * (HEAD_DIM ** -0.5)
        t_q = q0 + jnp.arange(SB_BLOCK)
        t_k = jnp.arange(kl)
        causal = t_k[None, :] < t_q[:, None]
        log_keep = jnp.where(causal, -jax.nn.softplus(z), 0.0)
        later = lax.cumsum(log_keep, axis=3, reverse=True) - log_keep
        a = jnp.where(causal, jnp.exp(jax.nn.log_sigmoid(z) + later), 0.0)
        outs.append(jnp.einsum('bhqk,bkhd->bqhd', a.astype(v.dtype), v[:, :kl]))
    o = jnp.concatenate(outs, axis=1).reshape(B, S, SB_HEADS * HEAD_DIM)
    return o @ w_o

def squared_relu_mlp(h, w1, w2):
    return jnp.square(jax.nn.relu(h @ w1)) @ w2

def setup_inputs(seed: int = 0) -> dict:
    key = jax.random.key(seed)
    ks = jax.random.split(key, 24)
    nrm = jax.random.normal
    f32 = jnp.float32
    D = D_MODEL
    x = nrm(ks[0], (BATCH, SEQ, D), f32)
    c = nrm(ks[1], (BATCH, D), f32)
    offsets = jax.random.randint(ks[2], (BATCH, 1), 0, MAX_POS_OFFSET, dtype=jnp.int32)
    positions = offsets + jnp.arange(SEQ, dtype=jnp.int32)[None, :]
    norm1_gain = 1.0 + 0.02 * nrm(ks[3], (DEPTH, D), f32)
    norm2_gain = 1.0 + 0.02 * nrm(ks[4], (DEPTH, D), f32)
    mod_w = nrm(ks[5], (DEPTH, D, 6 * D), f32) * (0.5 * D ** -0.5)
    mod_b = 0.02 * nrm(ks[6], (DEPTH, 6 * D), f32)
    swa_w_qkv = nrm(ks[7], (N_SWA_LAYERS, D, SWA_Q_WIDTH + 2 * SWA_KV_WIDTH), f32) * D ** -0.5
    swa_q_gain = 1.0 + 0.02 * nrm(ks[8], (N_SWA_LAYERS, HEAD_DIM), f32)
    swa_k_gain = 1.0 + 0.02 * nrm(ks[9], (N_SWA_LAYERS, HEAD_DIM), f32)
    swa_sinks = 0.5 * nrm(ks[10], (N_SWA_LAYERS, SWA_HEADS), f32)
    swa_w_o = nrm(ks[11], (N_SWA_LAYERS, SWA_Q_WIDTH, D), f32) * SWA_Q_WIDTH ** -0.5
    gmlp_w_uv = nrm(ks[12], (N_GMLP_LAYERS, D, 2 * GMLP_WIDTH), f32) * D ** -0.5
    gmlp_v_gain = 1.0 + 0.02 * nrm(ks[13], (N_GMLP_LAYERS, GMLP_WIDTH), f32)
    gmlp_w_s = nrm(ks[14], (N_GMLP_LAYERS, GMLP_GROUPS, GMLP_BLOCK, GMLP_BLOCK), f32) * GMLP_BLOCK ** -0.5
    gmlp_s_bias = 1.0 + 0.1 * nrm(ks[15], (N_GMLP_LAYERS, GMLP_GROUPS, GMLP_BLOCK), f32)
    gmlp_w_o = nrm(ks[16], (N_GMLP_LAYERS, GMLP_WIDTH, D), f32) * GMLP_WIDTH ** -0.5
    sb_w_qkv = nrm(ks[17], (N_SB_LAYERS, D, 3 * SB_HEADS * HEAD_DIM), f32) * D ** -0.5
    sb_w_o = nrm(ks[18], (N_SB_LAYERS, SB_HEADS * HEAD_DIM, D), f32) * (SB_HEADS * HEAD_DIM) ** -0.5
    mlp_w1 = nrm(ks[19], (DEPTH, D, MLP_HIDDEN), f32) * D ** -0.5
    mlp_w2 = nrm(ks[20], (DEPTH, MLP_HIDDEN, D), f32) * MLP_HIDDEN ** -0.5
    return {'x': x, 'c': c, 'positions': positions,
            'norm1_gain': norm1_gain, 'norm2_gain': norm2_gain, 'mod_w': mod_w, 'mod_b': mod_b,
            'swa_w_qkv': swa_w_qkv, 'swa_q_gain': swa_q_gain, 'swa_k_gain': swa_k_gain,
            'swa_sinks': swa_sinks, 'swa_w_o': swa_w_o,
            'gmlp_w_uv': gmlp_w_uv, 'gmlp_v_gain': gmlp_v_gain, 'gmlp_w_s': gmlp_w_s,
            'gmlp_s_bias': gmlp_s_bias, 'gmlp_w_o': gmlp_w_o,
            'sb_w_qkv': sb_w_qkv, 'sb_w_o': sb_w_o,
            'mlp_w1': mlp_w1, 'mlp_w2': mlp_w2}

def reference(x, c, positions, norm1_gain, norm2_gain, mod_w, mod_b,
              swa_w_qkv, swa_q_gain, swa_k_gain, swa_sinks, swa_w_o,
              gmlp_w_uv, gmlp_v_gain, gmlp_w_s, gmlp_s_bias, gmlp_w_o,
              sb_w_qkv, sb_w_o, mlp_w1, mlp_w2):
    cond = jax.nn.silu(c)
    for i in range(DEPTH):
        mod = (cond @ mod_w[i] + mod_b[i])[:, None, :]
        shift1, scale1, gate1, shift2, scale2, gate2 = jnp.split(mod, 6, axis=-1)
        h = rms_norm(x, norm1_gain[i]) * (1 + scale1) + shift1
        kind, slot = i % N_MIXERS, i // N_MIXERS
        if kind == 0:
            y = swa_sink_attention(h, positions, swa_w_qkv[slot], swa_q_gain[slot],
                                   swa_k_gain[slot], swa_sinks[slot], swa_w_o[slot])
        elif kind == 1:
            y = gmlp_spatial_gating(h, gmlp_w_uv[slot], gmlp_v_gain[slot], gmlp_w_s[slot],
                                    gmlp_s_bias[slot], gmlp_w_o[slot])
        else:
            y = stick_breaking_attention(h, sb_w_qkv[slot], sb_w_o[slot])
        x = x + gate1 * y
        h = rms_norm(x, norm2_gain[i]) * (1 + scale2) + shift2
        x = x + gate2 * squared_relu_mlp(h, mlp_w1[i], mlp_w2[i])
    return x


_drawn_inputs = setup_inputs


def setup_inputs(seed=0):
    import zlib

    import numpy as np

    out = dict(_drawn_inputs(seed))
    spreads = {}
    factors = {'norm1_gain': 8.0,
     'norm2_gain': 4.695,
     'swa_q_gain': 8.0,
     'swa_k_gain': 8.0,
     'swa_sinks': 8.0,
     'gmlp_v_gain': 8.0,
     'gmlp_s_bias': 2.919}
    for name, (base, spread) in spreads.items():
        noise = np.random.default_rng([zlib.crc32(name.encode()), seed]).standard_normal(out[name].shape)
        drawn = base * np.exp(spread * noise) if base else spread * noise
        out[name] = __import__('jax').numpy.asarray(drawn.astype(out[name].dtype))
    for name, factor in factors.items():
        out[name] = (out[name] * factor).astype(out[name].dtype)
    return out
```

```python
import concourse.bass as bass
from concourse import mybir
from contextlib import ExitStack

D = 1024
S = 1024
P = 128
KC = D // P
HALF = 512
HEADS, KV, HD = 16, 2, 64
GROUP = HEADS // KV
CHUNK = 64
NCH = S // CHUNK
PAD = CHUNK
HIDDEN = 4 * D
MLP_GROUPS = HIDDEN // D
GWIDTH = 2 * D
VCH = GWIDTH // P
EPS = 1e-6
MAGIC = 12582912.0
TWO_PI_1 = 6.28125
TWO_PI_2 = 0.0019350051879882812
TWO_PI_3 = 3.019915981956753e-07
PI = 3.1415925
TWO_PI = 6.283185307179586
LAG = 3

U_K, U_V, U_Q = 0, 1, 2
U_WO = U_Q + KC
U_MLP = [U_WO + KC, 0]
U_GV = U_MLP[0] + 2 * KC * MLP_GROUPS
U_GU = U_GV + VCH
U_MLP[1] = U_GU + 2 * 2 * KC
UNITS = U_MLP[1] + 2 * KC * MLP_GROUPS
SHIFT1, SCALE1, GATE1, SHIFT2, SCALE2, GATE2 = range(6)
PARTS = 12


def build(nc, x_in, c_in, pos_in, weights, mod_w, cols, mats, ws_in, bias_in, q_dram, v_dram, out):
    f32, f32r, i32 = mybir.dt.float32, mybir.dt.float32r, mybir.dt.int32
    ALU = mybir.AluOpType
    ACT = mybir.ActivationFunctionType
    X = mybir.AxisListType.X
    ctx = ExitStack()
    with ctx:
        def sb(name, shape, dt=f32, where=ctx):
            return where.enter_context(nc.sbuf_tensor(name, shape, dt))

        def sem(name):
            return ctx.enter_context(nc.semaphore(name))

        x = sb("x", [P, KC, S])
        w_raw = sb("w_raw", [P, 2, KC, P])
        w_hi = sb("w_hi", [P, 2, KC, P], f32r)
        w_lo = sb("w_lo", [P, 2, KC, P], f32r)
        ident = sb("ident", [P, P])
        ones = sb("ones", [P, P])
        colt = sb("colt", [P, cols.shape[1]])
        mod = sb("mod", [P, PARTS, KC])
        amp = sb("amp", [P, 4, KC])
        cond = sb("cond", [P, 3, KC])
        vmean = sb("vmean", [P, KC, 2])
        vscale = sb("vscale", [P, 2, KC])
        sink8 = sb("sink8", [P, 2 * 4])

        with ExitStack() as first:
            mod_first = sb("mod_first", [P, 2 * KC, S], where=first)
        h_hi = sb("h_hi", [P, KC, S], f32r)
        h_lo = sb("h_lo", [P, KC, S], f32r)

        with ExitStack() as attn:
            k1 = sb("k1", [P, KV, PAD + S], f32r, attn)
            k2 = sb("k2", [P, KV, PAD + S], f32r, attn)
            vt = sb("vt", [P, PAD + S], f32, attn)
            blocks = sb("blocks", [P, 2, P], f32, attn)
            with ExitStack() as kd_:
                kd = sb("kd", [P, KV, S], f32, kd_)
            v_s = sb("v_s", [P, NCH, 2, P], f32r, attn)
            with ExitStack() as rope:
                cos = sb("cos", [P, S], f32, rope)
                sin = sb("sin", [P, S], f32, rope)
                qa = sb("qa", [P, S], f32, rope)
                qb = sb("qb", [P, S], f32, rope)
                qr = sb("qr", [P, S], f32, rope)
                qx = sb("qx", [P, S], f32, rope)
            qf = sb("qf", [P, 2, HALF], f32, attn)
            q1 = sb("q1", [P, 2, HALF], f32r, attn)
            pr = sb("pr", [P, 2, 4, P + 1], f32, attn)
            pt_hi = sb("pt_hi", [P, 2, HALF], f32r, attn)
            pt_lo = sb("pt_lo", [P, 2, HALF], f32r, attn)
            v_w = sb("v_w", [P, 2, 2, P], f32r, attn)
            small = sb("small", [P, 2, 4, 4], f32, attn)
        with ExitStack() as late:
            mod_late = sb("mod_late", [P, 2 * KC, S], where=late)
        with ExitStack() as gv:
            v_out = sb("v_out", [P, 2, S], f32, gv)
            v_stat = sb("v_stat", [P, KC, VCH, 6], f32, gv)
        hid_hi = sb("hid_hi", [P, KC, S], f32r)
        hid_lo = sb("hid_lo", [P, KC, S], f32r)

        with ExitStack() as gu:
            wsg = sb("wsg", [P, P], f32, gu)
            wsg_hi = sb("wsg_hi", [P, P], f32r, gu)
            wsg_lo = sb("wsg_lo", [P, P], f32r, gu)
            biasg = sb("biasg", [P, P], f32, gu)
            with ExitStack() as vf_:
                vf = sb("vf", [P, KC, P], f32, vf_)
            vn_lo = sb("vn_lo", [P, KC, P], f32r, gu)
            vn_hi = sb("vn_hi", [P, KC, P], f32r, gu)
            u_t = sb("u_t", [P, S], f32, gu)
        mod_acc = sb("mod_acc", [P, S])
        tmp = sb("tmp", [P, 2, S])
        mod_t = sb("mod_t", [P, 2, S])
        sumsq = mod_t[:, 1, :]

        pp = [ctx.enter_context(nc.psum_tensor(f"pp{i}", [P, S], f32)) for i in range(4)]

        ngain = lambda n: colt[:, KC * n:KC * n + KC]
        mod_b = lambda part: colt[:, 4 * KC + KC * part:4 * KC + KC * part + KC]
        o = 4 * KC + PARTS * KC
        qgain_a, qgain_b, kgain = (colt[:, o + i:o + i + 1] for i in range(3))
        inv_freq = colt[:, o + 3:o + 4]
        eps = colt[:, o + 4:o + 5]
        vgain0 = o + 5
        sink0 = vgain0 + VCH

        raw_in = [sem("raw_in0"), sem("raw_in1")]
        hi_done, lo_done = sem("hi_done"), sem("lo_done")
        gemm = sem("gemm")
        evac = [sem("evac0"), sem("evac1")]
        c_ld, const_in = sem("c_ld"), sem("const_in")
        x_ld = [sem(f"x_ld{i}") for i in range(4)]
        mf_in = [sem(f"mf_in{i}") for i in range(2 * KC)]
        pos_s = sem("pos_s")
        dv = sem("dv")
        cexp, angle, trig = sem("cexp"), sem("angle"), sem("trig")
        mt_in = [sem("mt_in0"), sem("mt_in1")]
        mt_used = sem("mt_used")
        mf_used = sem("mf_used")
        mod_mm, mod_done = sem("mod_mm"), sem("mod_done")
        sq_done, ss_done = sem("sq_done"), sem("ss_done")
        ss_mm, sd_done, rs_done = sem("ss_mm"), sem("sd_done"), sem("rs_done")
        t_done, nh_done, h_done = sem("t_done"), sem("nh_done"), sem("h_done")
        q_sq, q_sum, q_ss, q_sd = sem("q_sq"), sem("q_sum"), sem("q_ss"), sem("q_sd")
        k_normed, k_swap, k_roped, kd_in = sem("k_normed"), sem("k_swap"), sem("k_roped"), sem("kd_in")
        k1_done, k2_done, vt_done = sem("k1_done"), sem("k2_done"), sem("vt_done")
        q_roped, q_out = sem("q_roped"), sem("q_out")
        pads = sem("pads")
        v_tr, v_hi_d, v_lo_d = sem("v_tr"), sem("v_hi_d"), sem("v_lo_d")
        qf_in = [sem("qf_in0"), sem("qf_in1")]
        q1h, q1l = sem("q1h"), sem("q1l")
        sc_mm, p_sub, p_exp, p_sum, p_norm = sem("sc_mm"), sem("p_sub"), sem("p_exp"), sem("p_sum"), sem("p_norm")
        p_tr, pth, ptl, vw, pv_mm, o_hi, o_lo = (sem(n) for n in ("p_tr", "pth", "ptl", "vw", "pv_mm", "o_hi", "o_lo"))
        p_tot, p_max = sem("p_tot"), sem("p_max")
        relu, hd_hi, hid = sem("relu"), sem("hd_hi"), sem("hid")
        vtr_mm, v_stats, v_copied = sem("vtr_mm"), sem("v_stats"), sem("v_copied")
        v_saved = [sem("v_saved0"), sem("v_saved1")]
        v_sd, v_sc, v_aggr, s_gain, ss_zero = sem("v_sd"), sem("v_sc"), sem("v_aggr"), sem("s_gain"), sem("ss_zero")
        vf_in, vn, vnh, vnl = sem("vf_in"), sem("vn"), sem("vnh"), sem("vnl")
        ws_ld, wsz, wsh, wsl = sem("ws_ld"), sem("wsz"), sem("wsh"), sem("wsl")
        sp_mm, t_mul, t_hi = sem("sp_mm"), sem("t_mul"), sem("t_hi")
        late_in = [sem("late_in0"), sem("late_in1")]
        acc_zero = sem("acc_zero")
        sink8_done = sem("sink8_done")
        saved = sem("saved")

        H_N = 2 * KC
        X_WO, X_MLP, X_G = 0, [KC, 7 * KC], 5 * KC
        HID_MLP = [2, 2 + KC * MLP_GROUPS + VCH]
        HID_G = 2 + KC * MLP_GROUPS
        RING_MLP, RING_GV = 2 * KC, 2 * KC + KC * MLP_GROUPS

        def static(*v):
            return all(isinstance(i, int) for i in v)

        block = ctx.enter_context(nc.Block())

        @block.sync
        def _(sp):
            sp.dma_start(cond[:, 0, :], c_in).then_inc(c_ld, 16)
            sp.dma_start(colt[:, :], cols).then_inc(const_in, 16)
            sp.dma_start(ones[:, :], mats[:, 1, :]).then_inc(const_in, 16)
            sp.dma_start(ident[:, :], mats[:, 0, :]).then_inc(const_in, 16)
            sp.dma_start(blocks[:, :, :], mats[:, 2:4, :]).then_inc(const_in, 16)
            sp.dma_start(qa[:, :].bitcast(i32), pos_in).then_inc(pos_s, 16)
            for i in range(4):
                sp.dma_start(x[:, 2 * i:2 * i + 2, :], x_in[:, 2 * i:2 * i + 2, :]).then_inc(x_ld[i], 16)
            for q in range(2 * KC):
                if q == KC:
                    for s in range(2):
                        sp.dma_start(w_raw[:, s, :, :], weights[s]).then_inc(raw_in[s], 16)
                sp.dma_start(mod_first[:, q, :], mod_w[q]).then_inc(mf_in[q], 16)

            def load_block(pair, s):
                sp.wait_ge(lo_done, pair * 2 + (s - 1))
                sp.dma_start(w_raw[:, s, :, :], weights[pair * 2 + s]).then_inc(raw_in[s], 16)

            def save_q(j):
                sp.wait_ge(q_roped, j + 1)
                for i in range(4):
                    head = 4 * (j % 2) + i
                    for part, src in ((0, qr), (1, qb)):
                        sp.dma_start(q_dram[:, j // 2, 32 * part:32 * part + 32, head, :].rearrange("n d t -> d n t"),
                                     src[32 * i:32 * i + 32, :].rearrange("d (n t) -> d n t", t=CHUNK)).then_inc(q_out, 16)

            with sp.Fori(1, 4) as pair:
                for s in range(2):
                    load_block(pair, s)
            for j in range(3):
                load_block(4 + j, 0)
                save_q(j)
                if j < 2:
                    load_block(4 + j, 1)
            load_block(6, 1)
            save_q(3)

            def load_q(t, n, g):
                if not static(t) or t >= 2:
                    sp.wait_ge(q1l, t - 1)
                for half in range(2):
                    sp.dma_start(qf[64 * half:64 * half + 64, g, :], q_dram[n, g]).then_inc(qf_in[g], 16)

            sp.wait_ge(q_out, 16 * 8 * 4)
            for g in range(KV):
                load_q(g, 0, g)
            with sp.Fori(1, NCH) as n:
                for g in range(KV):
                    load_q(n * 2 + g, n, g)

            with sp.Fori(7, UNITS // 2) as pair:
                for s in range(2):
                    load_block(pair, s)

            for n in range(KC):
                sp.wait_ge(evac[n % 2], (UNITS - KC + n) // 2 + 1)
                sp.dma_start(out[n], x[:, n, :]).then_inc(saved, 16)
            sp.wait_ge(saved, 16 * KC)

        @block.gpsimd
        def _(pool):
            def split_lo(pair, s):
                pool.wait_ge(hi_done, pair * 2 + (s + 1))
                nc.gpsimd.tensor_tensor(out=w_lo[:, s, :, :], in0=w_raw[:, s, :, :],
                                        in1=w_hi[:, s, :, :].bitcast(f32), op=ALU.subtract).then_inc(lo_done, 1)

            nc.gpsimd.memset(k1[:, :, 0:PAD].bitcast(f32), 0.0).then_inc(pads, 1)
            nc.gpsimd.memset(k2[:, :, 0:PAD].bitcast(f32), 0.0).then_inc(pads, 1)
            nc.gpsimd.memset(vt[:, 0:PAD], 0.0).then_inc(pads, 1)
            with pool.Fori(0, U_WO // 2 + 1) as pair:
                for s in range(2):
                    split_lo(pair, s)

            def q_low(t, g):
                if not static(t) or t >= 2:
                    pool.wait_ge(p_norm, t - 1)
                pool.wait_ge(q1h, t + 1)
                nc.gpsimd.tensor_tensor(out=q1[64:128, g, :], in0=qf[64:128, g, :],
                                        in1=q1[64:128, g, :].bitcast(f32), op=ALU.subtract).then_inc(q1l, 1)

            def normalise(t, g):
                pool.wait_ge(q1l, t + 2 if not static(t) else min(t + 2, 2 * NCH))
                pool.wait_ge(p_sum, t + 1)
                nc.gpsimd.tensor_tensor(out=pr[:, g, :, 0:P], in0=pr[:, g, :, 0:P],
                                        in1=small[:, g, 3, :].unsqueeze(2).to_broadcast([P, 4, P]),
                                        op=ALU.mult).then_inc(p_norm, 1)

            pool.wait_ge(lo_done, U_WO + 2)
            q_low(0, 0)
            q_low(1, 1)
            normalise(0, 0)
            with pool.Fori(1, NCH) as n:
                q_low(n * 2, 0)
                normalise(n * 2 - 1, 1)
                q_low(n * 2 + 1, 1)
                normalise(n * 2, 0)
            normalise(2 * NCH - 1, 1)

            with pool.Fori(U_WO // 2 + 1, U_GU // 2 + 1) as pair:
                for s in range(2):
                    split_lo(pair, s)

            with pool.Fori(0, 2) as kb:
                with pool.Fori(0, 4) as i:
                    for s in range(2):
                        pool.wait_ge(vnh, kb * KC + i * 2 + (s + 1))
                        nc.gpsimd.tensor_tensor(out=vn_lo[:, :, :], in0=vf[:, :, :], in1=vn_hi[:, :, :].bitcast(f32),
                                                op=ALU.subtract).then_inc(vnl, 1)
                        split_lo(kb * KC + i + (U_GU // 2 + 1), s)
                with pool.Fori(0, 4) as i:
                    for s in range(2):
                        split_lo(kb * KC + i + (U_GU // 2 + 5), s)
            with pool.Fori(U_MLP[1] // 2 + 1, UNITS // 2) as pair:
                for s in range(2):
                    split_lo(pair, s)

        @block.scalar
        def _(act):
            def split_hi(pair, s):
                act.wait_ge(raw_in[s], pair * 16 + 16)
                if not static(pair) or pair:
                    act.wait_ge(gemm, pair * 2 + (s - 1))
                nc.scalar.activation(w_hi[:, s, :, :], w_raw[:, s, :, :], ACT.Copy).then_inc(hi_done, 1)

            def load_mod(q, slot):
                if not static(q) or q >= 2:
                    act.wait_ge(mt_used, q - 1)
                late = 0 if static(q) and q < RING_MLP else 2 * KC
                act.dma_start(mod_t[:, slot, :], mod_w[q + (2 * KC + late)]).then_inc(mt_in[slot], 16)

            def square(k, s):
                nc.scalar.activation(tmp[:, s, :], x[:, bass.ds(k, 1), :].rearrange("p a s -> p (a s)"),
                                     ACT.Square).then_inc(sq_done, 1)

            def norm(n):
                act.wait_ge(ss_mm, n + 1)
                nc.scalar.activation(tmp[:, 0, :], pp[2][:, :], ACT.Sqrt, bias=eps, scale=1.0 / D).then_inc(sd_done, 1)
                act.wait_ge(mod_done, 3 * n + 2)
                with act.Fori(0, KC) as k:
                    for half in range(2):
                        cs = slice(HALF * half, HALF * half + HALF)
                        act.wait_ge(t_done, k * 2 + (H_N * n + half + 1))
                        nc.scalar.activation(h_hi[:, bass.ds(k, 1), cs].rearrange("p a s -> p (a s)"), pp[3][:, cs],
                                             ACT.Identity, bias=mod[:, 3 * n, bass.ds(k, 1)]).then_inc(nh_done, 1)

            act.wait_ge(c_ld, 16)
            nc.scalar.activation(cond[:, 1, :], cond[:, 0, :], ACT.Exp, scale=-1.0).then_inc(cexp, 1)
            for k in range(KC):
                if k % 2 == 0:
                    act.wait_ge(x_ld[k // 2], 16)
                if k >= 2:
                    act.wait_ge(ss_done, k - 1)
                square(k, k % 2)
            act.wait_ge(angle, 1)
            nc.scalar.activation(cos[:, :], cos[:, :], ACT.Sin).then_inc(trig, 1)
            nc.scalar.activation(sin[:, :], sin[:, :], ACT.Sin).then_inc(trig, 1)
            split_hi(0, 0)
            split_hi(0, 1)
            act.wait_ge(const_in, 64)
            norm(0)

            load_mod(0, 0)
            load_mod(1, 1)
            act.wait_ge(gemm, U_K + 1)
            split_hi(1, 0)
            nc.scalar.activation(qa[:, :], pp[0][:, :], ACT.Copy).then_inc(evac[0], 1)
            act.wait_ge(evac[0], 1)
            nc.scalar.activation(tmp[:, 0, :], qa[:, :], ACT.Square).then_inc(q_sq, 1)
            act.wait_ge(gemm, U_V + 1)
            split_hi(1, 1)
            nc.scalar.activation(vt[:, PAD:], pp[1][:, :], ACT.Copy).then_inc(evac[1], 1)
            load_mod(2, 0)
            load_mod(3, 1)
            act.wait_ge(q_ss, 1)
            nc.scalar.activation(qr[:, :], pp[2][:, :], ACT.Sqrt, bias=eps, scale=1.0 / HD).then_inc(q_sd, 1)
            act.wait_ge(k_normed, 1)
            act.dma_start(qb[0:64, :], qa[64:128, :]).then_inc(k_swap, 16)
            act.dma_start(qb[64:128, :], qa[0:64, :]).then_inc(k_swap, 16)
            load_mod(4, 0)
            load_mod(5, 1)
            act.wait_ge(k_roped, 2)
            for g in range(KV):
                for twice in range(2):
                    for part in range(2):
                        act.dma_start(kd[64 * twice + 32 * part:64 * twice + 32 * part + 32, g, :],
                                      qa[64 * part + 32 * g:64 * part + 32 * g + 32, :]).then_inc(kd_in, 16)
            act.wait_ge(kd_in, 16 * 8)
            nc.scalar.activation(k1[:, :, PAD:], kd[:, :, :], ACT.Copy).then_inc(k1_done, 1)

            for j in range(4):
                pair = U_Q // 2 + j
                act.wait_ge(gemm, 2 * pair + 1)
                split_hi(pair + 1, 0)
                if j:
                    act.wait_ge(q_roped, j)
                nc.scalar.activation(qa[:, :], pp[0][:, :], ACT.Copy).then_inc(evac[0], 1)
                if 6 + 3 * j < 2 * KC:
                    load_mod(6 + 3 * j, j % 2)
                act.wait_ge(evac[0], 2 + j)
                nc.scalar.activation(tmp[:, 0, :], qa[:, :], ACT.Square).then_inc(q_sq, 1)
                act.wait_ge(gemm, 2 * pair + 2)
                split_hi(pair + 1, 1)
                if j:
                    act.wait_ge(q_out, 16 * 8 * j)
                nc.scalar.activation(qb[:, :], pp[1][:, :], ACT.Copy).then_inc(evac[1], 1)
                act.wait_ge(evac[1], 2 + j)
                nc.scalar.activation(tmp[:, 1, :], qb[:, :], ACT.Square).then_inc(q_sq, 1)
                if 7 + 3 * j < 2 * KC:
                    load_mod(7 + 3 * j, (7 + 3 * j) % 2)
                act.wait_ge(k2_done, 1)
                act.wait_ge(v_tr, j + 1)
                nc.scalar.activation(v_s[:, 4 * j:4 * j + 4, 0, :],
                                     pp[3][:, 0:HALF].rearrange("p (n c) -> p n c", n=4), ACT.Copy).then_inc(v_hi_d, 1)
                if 8 + 3 * j < 2 * KC:
                    load_mod(8 + 3 * j, (8 + 3 * j) % 2)
                act.wait_ge(q_ss, j + 2)
                nc.scalar.activation(qr[:, :], pp[2][:, :], ACT.Sqrt, bias=eps, scale=1.0 / HD).then_inc(q_sd, 1)

            def q_high(t, n, g):
                act.wait_ge(qf_in[g], n * 32 + 32)
                if not static(t) or t >= 2:
                    act.wait_ge(sc_mm, t - 1)
                nc.scalar.activation(q1[:, g, :], qf[:, g, :], ACT.Copy).then_inc(q1h, 1)

            def probs_high(t, g):
                act.wait_ge(p_tr, t + 1)
                if not static(t) or t >= 2:
                    act.wait_ge(pv_mm, t - 1)
                nc.scalar.activation(pt_hi[:, g, :], pp[1][:, HALF * g:HALF * g + HALF], ACT.Copy).then_inc(pth, 1)

            def out_high(t, n, g):
                act.wait_ge(pv_mm, t + 1)
                rows = slice(64 * g, 64 * g + 64)
                nc.scalar.activation(h_hi[rows, :, bass.ds(n * CHUNK, CHUNK)],
                                     pp[2][rows, HALF * g:HALF * g + HALF].rearrange("p (h t) -> p h t", t=CHUNK),
                                     ACT.Copy).then_inc(o_hi, 1)

            def exps(t, g):
                act.wait_ge(p_sub, t + 1)
                nc.scalar.activation(pr[:, g, :, :], pr[:, g, :, :], ACT.Exp, scale=HD ** -0.5).then_inc(p_exp, 1)

            def window(t, n, e):
                if not static(t) or t >= 4:
                    act.wait_ge(pv_mm, t - 2)
                nc.scalar.activation(v_w[:, e, :, :], v_s[:, bass.ds(n, 1), :, :].rearrange("p a b c -> p (a b) c"),
                                     ACT.Copy).then_inc(vw, 1)

            def step(m, b):
                t = m * 4 + b
                if not static(t) or 2 <= t < 2 * NCH + 2:
                    probs_high(t - 2, b % 2)
                if not static(t) or 3 <= t:
                    out_high(t - 3, m * 2 + ((b + 1) // 2 - 2), (b + 1) % 2)
                if not static(t) or t < 2 * NCH:
                    exps(t, b % 2)
                    if b % 2 == 0:
                        window(t, m * 2 + b // 2, b // 2)
                if not static(t) or t + 1 < 2 * NCH:
                    q_high(t + 1, m * 2 + (b + 1) // 2, (b + 1) % 2)

            act.wait_ge(v_lo_d, 4)
            q_high(0, 0, 0)
            for b in range(4):
                step(0, b)
            with act.Fori(1, NCH // 2 - 1) as m:
                for b in range(4):
                    step(m, b)
            for b in range(7):
                step(NCH // 2 - 1 + b // 4, b % 4)

            def residual(pair0, first=0, count=4, split=True):
                with act.Fori(first, first + count) as i:
                    for s in range(2):
                        if split:
                            act.wait_ge(gemm, (i + pair0) * 2 + (s + 1))
                            split_hi(i + (pair0 + 1), s)
                        act.wait_ge(evac[s], i + (pair0 + 1))
                        square(i * 2 + s, s)

            act.wait_ge(o_lo, 2 * NCH)
            for part in range(2):
                act.dma_start(mod_late[:, KC * part:KC * part + KC, :],
                              mod_w[4 * KC + KC * part:4 * KC + KC * part + KC].rearrange("q p s -> p q s")).then_inc(late_in[part], 16)
            residual(U_WO // 2)
            norm(1)

            def mlp(layer):
                pair0 = U_MLP[layer] // 2
                c0 = KC * MLP_GROUPS * layer

                def group(g, last=False):
                    with act.Fori(0, 4) as i:
                        for s in range(2):
                            c = g * KC + i * 2 + s
                            pair = g * 8 + i + pair0
                            if layer == 0:
                                act.wait_ge(ss_done, g * KC + 2 * KC)
                                load_mod(c + RING_MLP, s)
                            act.wait_ge(gemm, pair * 2 + (s + 1))
                            act.wait_ge(hid, c + (HID_MLP[layer] - 1))
                            nc.scalar.activation(tmp[:, s, :], pp[s][:, :], ACT.Relu).then_inc(relu, 1)
                            split_hi(pair + 1, s)
                            act.wait_ge(evac[s], pair + 1)
                            nc.scalar.activation(hid_hi[:, bass.ds(i * 2 + s, 1), :].rearrange("p a s -> p (a s)"),
                                                 tmp[:, s, :], ACT.Copy).then_inc(hd_hi, 1)
                    if last:
                        residual(g * 8 + (pair0 + 4), 0, 3)
                        residual(g * 8 + (pair0 + 4), 3, 1, split=False)
                    else:
                        residual(g * 8 + (pair0 + 4))

                with act.Fori(0, MLP_GROUPS - layer) as g:
                    group(g)
                if layer:
                    group(MLP_GROUPS - 1, last=True)

            mlp(0)
            norm(2)

            def v_unit(i, s):
                c = i * 2 + s
                load_mod(c + RING_GV, s)
                act.wait_ge(gemm, c + (U_GV + 1))
                split_hi(i + (U_GV // 2 + 1), s)
                if not static(c) or c >= 2:
                    act.wait_ge(vtr_mm, c - 1)
                nc.scalar.activation(tmp[:, s, :], pp[s][:, :], ACT.Gelu).then_inc(evac[s], 1)

            def v_copy(c, s, before):
                act.wait_ge(v_stats, c + 1)
                if not static(before) or before:
                    act.wait_ge(v_saved[s], before * 16)
                nc.scalar.activation(v_out[:, s, :], pp[2][:, :], ACT.Copy).then_inc(v_copied, 1)
                act.wait_ge(v_copied, c + 1)
                act.dma_start(v_dram[c], v_out[:, s, :]).then_inc(v_saved[s], 16)

            v_unit(0, 0)
            v_unit(0, 1)
            v_copy(0, 0, 0)
            v_unit(1, 0)
            v_copy(1, 1, 0)
            v_unit(1, 1)
            v_copy(2, 0, 1)
            with act.Fori(2, VCH // 2) as i:
                v_unit(i, 0)
                v_copy(i * 2 - 1, 1, i - 1)
                v_unit(i, 1)
                v_copy(i * 2, 0, i)
            v_copy(VCH - 1, 1, VCH // 2 - 1)
            act.wait_ge(v_aggr, 1)
            nc.scalar.activation(vscale[:, 0, :], vmean[:, :, 1], ACT.Sqrt, bias=eps).then_inc(v_sd, 1)
            for s in range(2):
                act.wait_ge(v_saved[s], 16 * (VCH // 2))

            with act.Fori(0, 2) as kb:
                with act.Fori(0, 4) as i:
                    for s in range(2):
                        c = kb * KC + i * 2 + s
                        pair = kb * KC + i + U_GU // 2
                        act.wait_ge(ss_done, kb * KC + (2 + MLP_GROUPS) * KC)
                        act.wait_ge(hid, c + HID_G)
                        act.dma_start(vf[:, :, :], v_dram[c].rearrange("p (b f) -> p b f", b=KC)).then_inc(vf_in, 16)
                        if s == 0:
                            group = kb * 4 + i
                            act.dma_start(wsg[0:64, :], ws_in[group, 0:64, :]).then_inc(ws_ld, 16)
                            act.dma_start(wsg[64:128, 64:128], ws_in[group, 64:128, 64:128]).then_inc(ws_ld, 16)
                            act.dma_start(biasg[:, :], bias_in[group]).then_inc(ws_ld, 16)
                            act.wait_ge(wsz, 1)
                            act.wait_ge(ws_ld, group * 48 + 48)
                            nc.scalar.activation(wsg_hi[:, :], wsg[:, :], ACT.Copy).then_inc(wsh, 1)
                        act.wait_ge(vn, c + 1)
                        nc.scalar.activation(vn_hi[:, :, :], vf[:, :, :], ACT.Copy).then_inc(vnh, 1)
                        act.wait_ge(gemm, pair * 2 + (s + 1))
                        split_hi(pair + 1, s)
                        nc.scalar.activation(u_t[:, :], pp[s][:, :], ACT.Gelu).then_inc(evac[s], 1)
                        act.wait_ge(t_mul, c + 1)
                        nc.scalar.activation(hid_hi[:, bass.ds(i * 2 + s, 1), :].rearrange("p a s -> p (a s)"),
                                             pp[2][:, :], ACT.Copy).then_inc(t_hi, 1)
                residual(kb * KC + (U_GU // 2 + 4))
            norm(3)
            mlp(1)

        @block.vector
        def _(dve):
            chain = [0]

            def own(ins):
                chain[0] += 1
                ins.then_inc(dv, 1)
                dve.wait_ge(dv, chain[0])

            V = nc.vector

            def add_square(idx, s, first=False):
                dve.wait_ge(sq_done, idx + 1)
                dve.wait_ge(ss_done, idx) if not static(idx) or idx else None
                V.tensor_tensor(out=sumsq, in0=sumsq, in1=tmp[:, s, :], op=ALU.add).then_inc(ss_done, 1)

            def scale_add(tile, k, counter):
                V.scalar_tensor_tensor(out=mod_acc[:, :], in0=tile, scalar=cond[:, 2, bass.ds(k, 1)],
                                       in1=mod_acc[:, :], op0=ALU.mult, op1=ALU.add).then_inc(counter, 1)

            def mod_step(q, k, slot, loads):
                dve.wait_ge(mt_in[slot], loads * 16)
                if not static(q) or q:
                    dve.wait_ge(mt_used, q)
                scale_add(mod_t[:, slot, :], k, mt_used)

            def mod_part(part):
                dve.wait_ge(mod_mm, part + 1)
                V.tensor_tensor(out=mod[:, bass.ds(part, 1), :].rearrange("p a k -> p (a k)"),
                                in0=pp[3][:, HALF:HALF + KC], in1=colt[:, bass.ds(part * KC + 4 * KC, KC)],
                                op=ALU.add).then_inc(mod_done, 1)
                V.memset(mod_acc[:, :], 0.0).then_inc(acc_zero, 1)
                dve.wait_ge(acc_zero, part + 2)

            def norm(n):
                dve.wait_ge(mod_done, 3 * n + 2)
                own(V.scalar_tensor_tensor(out=amp[:, n, :], in0=mod[:, 3 * n + 1, :], scalar=1.0,
                                           in1=colt[:, KC * n:KC * n + KC], op0=ALU.add, op1=ALU.mult))
                dve.wait_ge(sd_done, n + 1)
                V.reciprocal(pp[2][:, :], tmp[:, 0, :]).then_inc(rs_done, 1)
                dve.wait_ge(rs_done, n + 1)

                def scaled(k, half):
                    cs = slice(HALF * half, HALF * half + HALF)
                    V.scalar_tensor_tensor(out=pp[3][:, cs], in0=x[:, bass.ds(k, 1), cs].rearrange("p a s -> p (a s)"),
                                           scalar=amp[:, n, bass.ds(k, 1)], in1=pp[2][:, cs],
                                           op0=ALU.mult, op1=ALU.mult).then_inc(t_done, 1)

                def low(k, half):
                    cs = slice(HALF * half, HALF * half + HALF)
                    dve.wait_ge(nh_done, k * 2 + (H_N * n + half + 1))
                    V.scalar_tensor_tensor(out=h_lo[:, bass.ds(k, 1), cs].rearrange("p a s -> p (a s)"),
                                           in0=pp[3][:, cs], scalar=mod[:, 3 * n, bass.ds(k, 1)],
                                           in1=h_hi[:, bass.ds(k, 1), cs].rearrange("p a s -> p (a s)").bitcast(f32),
                                           op0=ALU.add, op1=ALU.subtract).then_inc(h_done, 1)

                scaled(0, 0)
                scaled(0, 1)
                with dve.Fori(0, KC - 1) as k:
                    for half in range(2):
                        low(k, half)
                        dve.wait_ge(h_done, k * 2 + (H_N * n + half + 1))
                        scaled(k + 1, half)
                low(KC - 1, 0)
                low(KC - 1, 1)

            V.memset(vscale[:, 0, :], 0.0).then_inc(hid, 1)
            V.memset(vscale[:, 1, :], 0.0).then_inc(hid, 1)
            own(V.memset(sumsq, 0.0))
            V.memset(mod_acc[:, :], 0.0).then_inc(acc_zero, 1)
            dve.wait_ge(cexp, 1)
            own(V.tensor_scalar(cond[:, 1, :], cond[:, 1, :], 1.0, None, ALU.add))
            own(V.reciprocal(cond[:, 1, :], cond[:, 1, :]))
            own(V.tensor_tensor(out=cond[:, 2, :], in0=cond[:, 0, :], in1=cond[:, 1, :], op=ALU.mult))
            dve.wait_ge(pos_s, 16)
            dve.wait_ge(const_in, 64)
            V.tensor_scalar(sink8[:, :], colt[:, sink0:sink0 + 2 * 4], 8.0, None, ALU.mult).then_inc(sink8_done, 1)
            own(V.tensor_copy(cos[:, :], qa[:, :].bitcast(i32)))
            own(V.tensor_scalar(sin[:, :], cos[:, :], inv_freq, None, ALU.mult))
            own(V.tensor_scalar(qr[:, :], sin[:, :], 1.0 / TWO_PI, MAGIC, ALU.mult, ALU.add))
            own(V.tensor_scalar(qr[:, :], qr[:, :], MAGIC, None, ALU.subtract))
            for part in (TWO_PI_1, TWO_PI_2, TWO_PI_3):
                own(V.scalar_tensor_tensor(out=sin[:, :], in0=qr[:, :], scalar=-part, in1=sin[:, :],
                                           op0=ALU.mult, op1=ALU.add))
            own(V.tensor_scalar(sin[:, :], sin[:, :], -PI, PI, ALU.max, ALU.min))
            own(V.scalar_tensor_tensor(out=cos[:, :], in0=sin[:, :], scalar=-1.0, in1=sin[:, :],
                                       op0=ALU.mult, op1=ALU.max))
            V.tensor_scalar(cos[:, :], cos[:, :], -1.0, PI / 2, ALU.mult, ALU.add).then_inc(angle, 1)
            for k in range(KC):
                add_square(k, k % 2)
            for part in range(2):
                dve.wait_ge(acc_zero, part + 1)
                for k in range(KC):
                    q = part * KC + k
                    dve.wait_ge(mf_in[q], 16)
                    if q:
                        dve.wait_ge(mf_used, q)
                    scale_add(mod_first[:, q, :], k, mf_used)
                mod_part(part)
            norm(0)

            dve.wait_ge(trig, 2)
            mod_q = [0]

            def mods(count):
                for _ in range(count):
                    q = mod_q[0]
                    mod_step(q, q % KC, q % 2, q // 2 + 1)
                    mod_q[0] += 1

            mods(2)
            dve.wait_ge(q_sd, 1)
            own(V.reciprocal(qr[:, :], qr[:, :]))
            V.scalar_tensor_tensor(out=qa[:, :], in0=qa[:, :], scalar=kgain, in1=qr[:, :],
                                   op0=ALU.mult, op1=ALU.mult).then_inc(k_normed, 1)
            mods(2)
            dve.wait_ge(k_normed, 1)
            own(V.tensor_tensor(out=tmp[:, 0, :], in0=qa[:, :], in1=cos[:, :], op=ALU.mult))
            dve.wait_ge(k_swap, 32)
            own(V.tensor_tensor(out=tmp[:, 1, :], in0=qb[:, :], in1=sin[:, :], op=ALU.mult))
            for r, op in ((slice(0, 64), ALU.subtract), (slice(64, 128), ALU.add)):
                V.tensor_tensor(out=qa[r, :], in0=tmp[r, 0, :], in1=tmp[r, 1, :], op=op).then_inc(k_roped, 1)
            dve.wait_ge(k1_done, 1)
            V.tensor_tensor(out=k2[:, :, PAD:], in0=kd[:, :, :], in1=k1[:, :, PAD:].bitcast(f32),
                            op=ALU.subtract).then_inc(k2_done, 1)
            for j in range(4):
                mods(1)
                dve.wait_ge(q_sq, 1 + 2 * (j + 1))
                V.tensor_tensor(out=tmp[:, 0, :], in0=tmp[:, 0, :], in1=tmp[:, 1, :], op=ALU.add).then_inc(q_sum, 1)
                if j == 1:
                    mod_part(2)
                mods(1)
                dve.wait_ge(v_hi_d, j + 1)
                V.tensor_tensor(out=v_s[:, 4 * j:4 * j + 4, 1, :],
                                in0=pp[3][:, 0:HALF].rearrange("p (n c) -> p n c", n=4),
                                in1=v_s[:, 4 * j:4 * j + 4, 0, :].bitcast(f32), op=ALU.subtract).then_inc(v_lo_d, 1)
                mods(1)
                dve.wait_ge(q_sd, j + 2)
                own(V.reciprocal(qr[:, :], qr[:, :]))
                own(V.tensor_tensor(out=tmp[:, 0, :], in0=cos[:, :], in1=qr[:, :], op=ALU.mult))
                own(V.tensor_tensor(out=tmp[:, 1, :], in0=sin[:, :], in1=qr[:, :], op=ALU.mult))

                def turn(dst, src, gain, by):
                    own(V.scalar_tensor_tensor(out=dst[:, :], in0=src[:, :], scalar=gain, in1=tmp[:, by, :],
                                               op0=ALU.mult, op1=ALU.mult))

                turn(qx, qb, qgain_b, 1)
                turn(qr, qa, qgain_a, 0)
                turn(qb, qb, qgain_b, 0)
                turn(qa, qa, qgain_a, 1)
                own(V.tensor_tensor(out=qr[:, :], in0=qr[:, :], in1=qx[:, :], op=ALU.subtract))
                V.tensor_tensor(out=qb[:, :], in0=qb[:, :], in1=qa[:, :], op=ALU.add).then_inc(q_roped, 1)
            mod_part(3)

            def sums(t, g):
                dve.wait_ge(p_exp, t + 1)
                if not static(t) or t >= 2:
                    dve.wait_ge(p_norm, t - 1)
                V.tensor_reduce(out=small[:, g, 2, :], in_=pr[:, g, :, :], axis=X, op=ALU.add).then_inc(p_tot, 1)
                dve.wait_ge(p_tot, t + 1)
                V.reciprocal(small[:, g, 3, :], small[:, g, 2, :]).then_inc(p_sum, 1)

            def probs_low(t, g):
                dve.wait_ge(pth, t + 1)
                V.tensor_tensor(out=pt_lo[:, g, :], in0=pp[1][:, HALF * g:HALF * g + HALF],
                                in1=pt_hi[:, g, :].bitcast(f32), op=ALU.subtract).then_inc(ptl, 1)

            def maxima(t, g):
                lo = PAD if static(t) and t < 2 else 0
                sc = pp[0][:, HALF * g:HALF * g + HALF].rearrange("p (r k) -> p r k", k=P)
                dve.wait_ge(sc_mm, t + 1)
                if not static(t) or t >= 2:
                    dve.wait_ge(p_tr, t - 1)
                V.tensor_reduce(out=small[:, g, 0, :], in_=sc[:, :, lo:], axis=X, op=ALU.max).then_inc(p_max, 1)
                dve.wait_ge(p_max, t * 2 + 1)
                V.tensor_tensor(out=small[:, g, 1, :], in0=small[:, g, 0, :], in1=sink8[:, 4 * g:4 * g + 4],
                                op=ALU.max).then_inc(p_max, 1)
                dve.wait_ge(p_max, t * 2 + 2)
                if lo:
                    V.memset(pr[:, g, :, 0:lo], -1.0e4)
                V.tensor_tensor(out=pr[:, g, :, P:P + 1], in0=sink8[:, 4 * g:4 * g + 4].unsqueeze(2),
                                in1=small[:, g, 1, :].unsqueeze(2), op=ALU.subtract)
                V.tensor_tensor(out=pr[:, g, :, lo:P], in0=sc[:, :, lo:],
                                in1=small[:, g, 1, :].unsqueeze(2).to_broadcast([P, 4, P - lo]),
                                op=ALU.subtract).then_inc(p_sub, 1)

            def out_low(t, n, g):
                rows = slice(64 * g, 64 * g + 64)
                cs = bass.ds(n * CHUNK, CHUNK)
                dve.wait_ge(o_hi, t + 1)
                V.tensor_tensor(out=h_lo[rows, :, cs],
                                in0=pp[2][rows, HALF * g:HALF * g + HALF].rearrange("p (h t) -> p h t", t=CHUNK),
                                in1=h_hi[rows, :, cs].bitcast(f32), op=ALU.subtract).then_inc(o_lo, 1)

            def step(m, b):
                t = m * 4 + b
                if not static(t) or 1 <= t < 2 * NCH + 1:
                    sums(t - 1, (b + 1) % 2)
                if not static(t) or t < 2 * NCH:
                    maxima(t, b % 2)
                if not static(t) or 2 <= t < 2 * NCH + 2:
                    probs_low(t - 2, b % 2)
                if not static(t) or 3 <= t:
                    out_low(t - 3, m * 2 + ((b + 1) // 2 - 2), (b + 1) % 2)

            dve.wait_ge(sink8_done, 1)
            for b in range(4):
                step(0, b)
            with dve.Fori(1, NCH // 2 - 1) as m:
                for b in range(4):
                    step(m, b)
            for b in range(7):
                step(NCH // 2 - 1 + b // 4, b % 4)

            def residual(pair0, n0, gate, first=0, count=4, late=None, zeroed=None):
                with dve.Fori(first, first + count) as i:
                    for s in range(2):
                        xn = x[:, bass.ds(i * 2 + s, 1), :].rearrange("p a s -> p (a s)")
                        dve.wait_ge(gemm, (i + pair0) * 2 + (s + 1))
                        V.scalar_tensor_tensor(out=xn, in0=pp[s][:, :], scalar=mod[:, gate, bass.ds(i * 2 + s, 1)],
                                               in1=xn, op0=ALU.mult, op1=ALU.add).then_inc(evac[s], 1)
                        if zeroed is not None:
                            dve.wait_ge(ss_zero, zeroed)
                        if late is not None:
                            for r in range(2):
                                k = (i - first) * 4 + (2 * s + r)
                                dve.wait_ge(mf_used, k + (2 * KC + KC * late))
                                scale_add(mod_late[:, bass.ds(k + KC * late, 1), :].rearrange("p a s -> p (a s)"), k, mf_used)
                        add_square(i * 2 + (n0 + KC + s), s)

            own(V.memset(sumsq, 0.0))
            for late in range(2):
                dve.wait_ge(late_in[late], 16)
                residual(U_WO // 2, X_WO, GATE1, 2 * late, 2, late)
                mod_part(4 + late)
            norm(1)

            def mlp(layer):
                pair0 = U_MLP[layer] // 2
                c0 = KC * MLP_GROUPS * layer
                with dve.Fori(0, MLP_GROUPS) as g:
                    with dve.Fori(0, 4) as i:
                        for s in range(2):
                            c = g * KC + i * 2 + s
                            if layer == 0:
                                mod_step(c + RING_MLP, i * 2 + s, s, g * 4 + i + (RING_MLP // 2 + 1))
                            dve.wait_ge(relu, c + (c0 + 1))
                            V.scalar_tensor_tensor(out=tmp[:, s, :], in0=pp[s][:, :], scalar=0.0, in1=tmp[:, s, :],
                                                   op0=ALU.max, op1=ALU.mult).then_inc(evac[s], 1)
                            dve.wait_ge(hd_hi, c + (c0 + 1))
                            V.tensor_tensor(out=hid_lo[:, bass.ds(i * 2 + s, 1), :].rearrange("p a s -> p (a s)"),
                                            in0=tmp[:, s, :],
                                            in1=hid_hi[:, bass.ds(i * 2 + s, 1), :].rearrange("p a s -> p (a s)").bitcast(f32),
                                            op=ALU.subtract).then_inc(hid, 1)
                    if layer == 0:
                        mod_part(g + 6)
                    V.memset(sumsq, 0.0).then_inc(ss_zero, 1)
                    residual(g * 8 + (pair0 + 4), g * KC + X_MLP[layer], 6 * layer + GATE2,
                             zeroed=g + (1 + layer * (MLP_GROUPS + 2)))

            mlp(0)
            norm(2)

            for half in range(2):
                with dve.Fori(4 * half, 4 * half + 4) as i:
                    for s in range(2):
                        c = i * 2 + s
                        mod_step(c + RING_GV, c - KC * half, s, i + (RING_GV // 2 + 1))
                        dve.wait_ge(vtr_mm, c + 1)
                        for b in range(KC):
                            ins = V.bn_stats(v_stat[:, b, bass.ds(c, 1), :].rearrange("p a s -> p (a s)"),
                                             pp[2][:, P * b:P * b + P])
                        ins.then_inc(v_stats, 1)
                mod_part(10 + half)
            dve.wait_ge(v_stats, VCH)
            for b in range(KC):
                ins = V.bn_aggr(vmean[:, b, :], v_stat[:, b, :, :].rearrange("p c s -> p (c s)"))
            ins.then_inc(v_aggr, 1)
            dve.wait_ge(v_sd, 1)
            own(V.reciprocal(vscale[:, 0, :], vscale[:, 0, :]))
            V.scalar_tensor_tensor(out=vscale[:, 1, :], in0=vmean[:, :, 0], scalar=-1.0, in1=vscale[:, 0, :],
                                   op0=ALU.mult, op1=ALU.mult).then_inc(v_sc, 1)
            dve.wait_ge(v_sc, 1)
            V.memset(wsg[64:128, 0:64], 0.0).then_inc(wsz, 1)

            with dve.Fori(0, 2) as kb:
                with dve.Fori(0, 4) as i:
                    for s in range(2):
                        c = kb * KC + i * 2 + s
                        pair = kb * KC + i + U_GU // 2
                        dve.wait_ge(vf_in, c * 16 + 16)
                        for b in range(KC):
                            ins = V.tensor_scalar(vf[:, b, :], vf[:, b, :], vscale[:, 0, b:b + 1],
                                                  vscale[:, 1, b:b + 1], ALU.mult, ALU.add)
                        ins.then_inc(vn, 1)
                        if s == 0:
                            dve.wait_ge(wsh, kb * 4 + i + 1)
                            V.tensor_tensor(out=wsg_lo[:, :], in0=wsg[:, :], in1=wsg_hi[:, :].bitcast(f32),
                                            op=ALU.subtract).then_inc(wsl, 1)
                        mixed = pp[2][:, :].rearrange("p (b t) -> p b t", b=KC)
                        dve.wait_ge(sp_mm, c + 1)
                        V.scalar_tensor_tensor(out=mixed, in0=mixed, scalar=colt[:, bass.ds(c + vgain0, 1)],
                                               in1=biasg[:, :].unsqueeze(1).to_broadcast([P, KC, P]),
                                               op0=ALU.mult, op1=ALU.add).then_inc(s_gain, 1)
                        dve.wait_ge(s_gain, c + 1)
                        dve.wait_ge(evac[s], pair + 1)
                        V.tensor_tensor(out=pp[2][:, :], in0=pp[2][:, :], in1=u_t[:, :], op=ALU.mult).then_inc(t_mul, 1)
                        dve.wait_ge(t_hi, c + 1)
                        V.tensor_tensor(out=hid_lo[:, bass.ds(i * 2 + s, 1), :].rearrange("p a s -> p (a s)"),
                                        in0=pp[2][:, :],
                                        in1=hid_hi[:, bass.ds(i * 2 + s, 1), :].rearrange("p a s -> p (a s)").bitcast(f32),
                                        op=ALU.subtract).then_inc(hid, 1)
                V.memset(sumsq, 0.0).then_inc(ss_zero, 1)
                residual(kb * KC + (U_GU // 2 + 4), kb * KC + X_G, 6 + GATE1, zeroed=kb + (MLP_GROUPS + 1))
            norm(3)
            mlp(1)

        @block.tensor
        def _(pe):
            T = nc.tensor

            def ready(pair, s):
                pe.wait_ge(lo_done, pair * 2 + (s + 1))
                if not static(pair) or pair:
                    pe.wait_ge(evac[s], pair)

            def products(s, k, hi, lo):
                for w, parts in ((w_hi, (hi, lo)), (w_lo, (hi,))):
                    for r in parts:
                        for half in range(2):
                            cs = slice(HALF * half, HALF * half + HALF)
                            last = T.matmul(pp[s][:, cs], w[:, s, k, :], r[:, k, cs],
                                            start=(k == 0 and w is w_hi and r is hi),
                                            stop=(k == KC - 1 and w is w_lo))
                return last

            def unit(pair, s, hi, lo, chunk_ready=None, hook=None):
                ready(pair, s)
                for k in range(KC):
                    if chunk_ready:
                        pe.wait_ge(chunk_ready[0], chunk_ready[1] + k)
                    last = products(s, k, hi, lo)
                    if hook and k == 4:
                        hook()
                last.then_inc(gemm, 1)

            def normed_pair(pair, n):
                ready(pair, 0)
                ready(pair, 1)
                for k in range(KC + LAG):
                    if k < KC:
                        pe.wait_ge(h_done, H_N * n + 2 * k + 2)
                        last = products(0, k, h_hi, h_lo)
                        if k == KC - 1:
                            last.then_inc(gemm, 1)
                    if k >= LAG:
                        last = products(1, k - LAG, h_hi, h_lo)
                last.then_inc(gemm, 1)

            def mod_columns(part, counter, count):
                pe.wait_ge(counter, count)
                for k in range(KC):
                    last = T.matmul(pp[3][:, HALF + k:HALF + k + 1], mod_acc[:, P * k:P * k + P], ones[:, 0:1],
                                    start=True, stop=True)
                last.then_inc(mod_mm, 1)

            def sum_squares(n, squares):
                pe.wait_ge(ss_done, squares)
                for half in range(2):
                    cs = slice(HALF * half, HALF * half + HALF)
                    last = T.matmul(pp[2][:, cs], ones[:, :], mod_t[:, 1, cs], start=True, stop=True)
                last.then_inc(ss_mm, 1)

            pe.wait_ge(const_in, 64)
            sum_squares(0, KC)
            mod_columns(0, mf_used, KC)
            mod_columns(1, mf_used, 2 * KC)

            def head_squares(j):
                if j < 0:
                    pe.wait_ge(q_sq, 1)
                    pe.wait_ge(rs_done, 1)
                else:
                    pe.wait_ge(q_sum, j + 1)
                    pe.wait_ge(q_sd, j + 1)
                for half in range(2):
                    cs = slice(HALF * half, HALF * half + HALF)
                    last = T.matmul(pp[2][:, cs], blocks[:, 1 if j < 0 else 0, :], tmp[:, 0, cs], start=True, stop=True)
                last.then_inc(q_ss, 1)

            normed_pair(0, 0)
            for j in range(4):
                unit(1 + j, 0, h_hi, h_lo, hook=lambda: head_squares(j - 1))
                unit(1 + j, 1, h_hi, h_lo)
                if j == 1:
                    mod_columns(2, mt_used, KC)
                pe.wait_ge(evac[1], 1)
                pe.wait_ge(pads, 3)
                if j:
                    pe.wait_ge(v_lo_d, j)
                for r in range(4):
                    n = 4 * j + r
                    last = T.transpose(pp[3][:, P * r:P * r + P], vt[:, CHUNK * n:CHUNK * n + P], ident[:, :])
                last.then_inc(v_tr, 1)
            head_squares(3)
            mod_columns(3, mt_used, 2 * KC)

            def scores(t, n, g):
                pe.wait_ge(q1l, t + 1)
                if not static(t) or t >= 2:
                    pe.wait_ge(p_sub, t - 1)
                cs = bass.ds(n * CHUNK, P)
                for r in range(4):
                    for kk in (k1, k2):
                        last = T.matmul(pp[0][:, HALF * g + P * r:HALF * g + P * r + P], q1[:, g, P * r:P * r + P],
                                        kk[:, g, cs], start=kk is k1, stop=kk is k2)
                last.then_inc(sc_mm, 1)

            def turn(t, g):
                pe.wait_ge(p_norm, t + 1)
                if not static(t) or t >= 2:
                    pe.wait_ge(ptl, t - 1)
                for r in range(4):
                    last = T.transpose(pp[1][:, HALF * g + P * r:HALF * g + P * r + P], pr[:, g, r, 0:P], ident[:, :])
                last.then_inc(p_tr, 1)

            def mix(t, n, g, e):
                pe.wait_ge(ptl, t + 1)
                pe.wait_ge(vw, n + 1)
                if not static(t) or t >= 2:
                    pe.wait_ge(o_lo, t - 1)
                dst = pp[2][:, HALF * g:HALF * g + HALF]
                T.matmul(dst, v_w[:, e, 0, :], pt_hi[:, g, :], start=True, stop=False)
                T.matmul(dst, v_w[:, e, 0, :], pt_lo[:, g, :], start=False, stop=False)
                T.matmul(dst, v_w[:, e, 1, :], pt_hi[:, g, :], start=False, stop=True).then_inc(pv_mm, 1)

            def step(m, b):
                t = m * 4 + b
                if not static(t) or t < 2 * NCH:
                    scores(t, m * 2 + b // 2, b % 2)
                if not static(t) or 2 <= t < 2 * NCH + 2:
                    mix(t - 2, m * 2 + (b // 2 - 1), b % 2, (b // 2 + 1) % 2)
                if not static(t) or 1 <= t < 2 * NCH + 1:
                    turn(t - 1, (b + 1) % 2)

            pe.wait_ge(k2_done, 1)
            pe.wait_ge(evac[0], U_WO // 2)
            pe.wait_ge(evac[1], U_WO // 2)
            pe.wait_ge(q_sd, 5)
            for b in range(4):
                step(0, b)
            with pe.Fori(1, NCH // 2 - 1) as m:
                for b in range(4):
                    step(m, b)
            for b in range(6):
                step(NCH // 2 - 1 + b // 4, b % 4)

            pe.wait_ge(o_lo, 2 * NCH)
            for late in range(2):
                with pe.Fori(U_WO // 2 + 2 * late, U_WO // 2 + 2 * late + 2) as pair:
                    for s in range(2):
                        unit(pair, s, h_hi, h_lo)
                mod_columns(4 + late, mf_used, 3 * KC + KC * late)
            sum_squares(1, 2 * KC)

            def h_units(pair0, first, count=4):
                with pe.Fori(first, count) as i:
                    for s in range(2):
                        unit(i + pair0, s, h_hi, h_lo)

            def hid_units(pair0, hid0, after=None):
                unit(pair0, 0, hid_hi, hid_lo, (hid, hid0 + 1))
                if after:
                    after()
                unit(pair0, 1, hid_hi, hid_lo)
                with pe.Fori(1, 4) as i:
                    for s in range(2):
                        unit(i + pair0, s, hid_hi, hid_lo)

            def mlp(layer):
                pair0 = U_MLP[layer] // 2
                normed_pair(pair0, 2 * layer + 1)
                h_units(pair0, 1)

                def down(g):
                    columns = (lambda: mod_columns(g + 6, mt_used, g * KC + (RING_MLP + KC))) if layer == 0 else None
                    hid_units(g * 8 + (pair0 + 4), g * KC + HID_MLP[layer], columns)

                down(0)
                with pe.Fori(1, MLP_GROUPS) as g:
                    h_units(g * 8 + pair0, 0)
                    down(g)

            mlp(0)
            sum_squares(2, (2 + MLP_GROUPS) * KC)

            def v_turn(c, s, pair):
                pe.wait_ge(evac[s], pair + 1)
                if not static(c) or c:
                    pe.wait_ge(v_copied, c)
                for b in range(KC):
                    last = T.transpose(pp[2][:, P * b:P * b + P], tmp[:, s, P * b:P * b + P], ident[:, :])
                last.then_inc(vtr_mm, 1)

            gv = U_GV // 2
            normed_pair(gv, 2)
            v_turn(0, 0, gv)
            with pe.Fori(1, 4) as i:
                unit(i + gv, 0, h_hi, h_lo)
                v_turn(i * 2 - 1, 1, i + (gv - 1))
                unit(i + gv, 1, h_hi, h_lo)
                v_turn(i * 2, 0, i + gv)
            unit(gv + 4, 0, h_hi, h_lo)
            v_turn(7, 1, gv + 3)
            mod_columns(10, mt_used, RING_GV + KC)
            unit(gv + 4, 1, h_hi, h_lo)
            v_turn(8, 0, gv + 4)
            with pe.Fori(5, 8) as i:
                unit(i + gv, 0, h_hi, h_lo)
                v_turn(i * 2 - 1, 1, i + (gv - 1))
                unit(i + gv, 1, h_hi, h_lo)
                v_turn(i * 2, 0, i + gv)
            v_turn(VCH - 1, 1, gv + 7)
            mod_columns(11, mt_used, RING_GV + 2 * KC)

            def blend(c, group):
                pe.wait_ge(vnl, c + 1)
                pe.wait_ge(wsl, group + 1)
                pe.wait_ge(hid, c + HID_G)
                for b in range(KC):
                    dst = pp[2][:, P * b:P * b + P]
                    T.matmul(dst, vn_hi[:, b, :], wsg_hi[:, :], start=True, stop=False)
                    T.matmul(dst, vn_hi[:, b, :], wsg_lo[:, :], start=False, stop=False)
                    last = T.matmul(dst, vn_lo[:, b, :], wsg_hi[:, :], start=False, stop=True)
                last.then_inc(sp_mm, 1)

            with pe.Fori(0, 2) as kb:
                with pe.Fori(0, 4) as i:
                    for s in range(2):
                        unit(kb * KC + i + U_GU // 2, s, h_hi, h_lo)
                        blend(kb * KC + i * 2 + s, kb * 4 + i)
                hid_units(kb * KC + (U_GU // 2 + 4), kb * KC + HID_G)
            sum_squares(3, (4 + MLP_GROUPS) * KC)
            mlp(1)


def kernel(x, c, positions, norm1_gain, norm2_gain, mod_w, mod_b, swa_w_qkv, swa_q_gain, swa_k_gain,
           swa_sinks, swa_w_o, gmlp_w_uv, gmlp_v_gain, gmlp_w_s, gmlp_s_bias, gmlp_w_o, sb_w_qkv, sb_w_o,
           mlp_w1, mlp_w2):
    import numpy as np
    import concourse.bacc as bacc
    from concourse.bass_utils import run_bass_kernel_spmd

    def blocks(w):
        k, n = w.shape
        return w.reshape(k // D, KC, P, n // P, P).transpose(0, 3, 2, 1, 4)

    def columns(v):
        return v.reshape(-1, P).T

    f = {k: np.asarray(v) for k, v in dict(
        x=x, c=c, positions=positions, n1=norm1_gain, n2=norm2_gain, mw=mod_w, mb=mod_b, qkv=swa_w_qkv, qg=swa_q_gain,
        kg=swa_k_gain, sinks=swa_sinks, wo=swa_w_o, uv=gmlp_w_uv, vg=gmlp_v_gain, ws=gmlp_w_s, sb=gmlp_s_bias,
        go=gmlp_w_o, w1=mlp_w1, w2=mlp_w2).items()}
    wq = f["qkv"][0][:, :HEADS * HD].reshape(D, 4, 4, 2, HD // 2).transpose(0, 1, 3, 2, 4).reshape(D, HEADS * HD)
    wk = f["qkv"][0][:, HEADS * HD:HEADS * HD + P].reshape(D, KV, 2, HD // 2).transpose(0, 2, 1, 3).reshape(D, P)
    wv = f["qkv"][0][:, HEADS * HD + P:]
    wo = f["wo"][0].reshape(KV, GROUP, HD, D).transpose(1, 0, 2, 3).reshape(D, D)
    order = [blocks(wk)[0], blocks(wv)[0], blocks(wq)[0], blocks(wo)[0]]

    def mlp_blocks(layer):
        up, down = blocks(f["w1"][layer])[0], blocks(f["w2"][layer])
        for g in range(MLP_GROUPS):
            order.extend((up[KC * g:KC * g + KC], down[g]))

    mlp_blocks(0)
    uv, go = blocks(f["uv"][0])[0], blocks(f["go"][0])
    order.append(uv[VCH:])
    for kb in range(2):
        order.extend((uv[KC * kb:KC * kb + KC], go[kb]))
    mlp_blocks(1)

    half = np.concatenate([f["qg"][0][:HD // 2]] * 4), np.concatenate([f["qg"][0][HD // 2:]] * 4)
    kgain = np.concatenate([f["kg"][0][:HD // 2]] * 2 + [f["kg"][0][HD // 2:]] * 2)
    freq = (10000.0 ** (-np.arange(0, HD, 2) / HD)).astype(np.float32)
    sinks = np.repeat(f["sinks"][0].reshape(KV * 4, 2).T, CHUNK, axis=0)
    cols = np.concatenate(
        [columns(g) for g in (f["n1"][0], f["n2"][0], f["n1"][1], f["n2"][1])]
        + [columns(f["mb"].reshape(-1))]
        + [a[:, None] for a in (half[0], half[1], kgain, np.tile(freq, 4), np.full(P, EPS, np.float32))]
        + [columns(f["vg"][0]), sinks], axis=1)
    r = np.arange(P)
    mats = np.stack([np.eye(P), np.ones((P, P)), r[:, None] // 32 == r // 32,
                     (r[:, None] // 32) % 2 == (r // 32) % 2], axis=1).astype(np.float32)
    arrays = {
        "x_in": f["x"][0].T.reshape(KC, P, S).transpose(1, 0, 2),
        "c_in": columns(f["c"][0]),
        "pos_in": np.broadcast_to(f["positions"][0], (P, S)),
        "weights": np.concatenate(order),
        "mod_w": f["mw"].reshape(2, KC, P, 6, D).transpose(0, 3, 1, 2, 4).reshape(PARTS * KC, P, D),
        "cols": cols,
        "mats": mats,
        "ws_in": f["ws"][0].transpose(0, 2, 1),
        "bias_in": np.broadcast_to(f["sb"][0][:, None, :], (KC, P, P)),
    }
    arrays = {k: np.ascontiguousarray(v) for k, v in arrays.items()}
    nc = bacc.Bacc("TRN2", target_bir_lowering=False, num_devices=1)
    dram = {k: nc.dram_tensor(k, a.shape, mybir.dt.from_np(a.dtype), kind="ExternalInput").ap() for k, a in arrays.items()}
    q_dram = nc.dram_tensor("q_dram", (NCH, KV, HD, GROUP, CHUNK), mybir.dt.float32, kind="Internal").ap()
    v_dram = nc.dram_tensor("v_dram", (VCH, P, S), mybir.dt.float32, kind="Internal").ap()
    out = nc.dram_tensor("out", (KC, P, S), mybir.dt.float32, kind="ExternalOutput").ap()
    build(nc, q_dram=q_dram, v_dram=v_dram, out=out, **dram)
    got = run_bass_kernel_spmd(nc, [arrays], core_ids=[0]).results[0]["out"]
    return np.ascontiguousarray(got.reshape(D, S).T)[None]
```

```python
import concourse.bass as bass
from concourse import mybir
from contextlib import ExitStack

D = 1024
S = 1024
P = 128
KC = D // P
HALF = 512
HEADS, KV, HD = 16, 2, 64
GROUP = HEADS // KV
CHUNK = 64
NCH = S // CHUNK
PAD = CHUNK
HIDDEN = 4 * D
MLP_GROUPS = HIDDEN // D
GWIDTH = 2 * D
VCH = GWIDTH // P
EPS = 1e-6
MAGIC = 12582912.0
TWO_PI_1 = 6.28125
TWO_PI_2 = 0.0019350051879882812
TWO_PI_3 = 3.019915981956753e-07
PI = 3.1415925
TWO_PI = 6.283185307179586
LAG = 3

U_K, U_V, U_Q = 0, 1, 2
U_WO = U_Q + KC
U_MLP = [U_WO + KC, 0]
U_GV = U_MLP[0] + 2 * KC * MLP_GROUPS
U_GU = U_GV + VCH
U_MLP[1] = U_GU + 2 * 2 * KC
UNITS = U_MLP[1] + 2 * KC * MLP_GROUPS
SHIFT1, SCALE1, GATE1, SHIFT2, SCALE2, GATE2 = range(6)
PARTS = 12


def build(nc, x_in, c_in, pos_in, weights, mod_w, cols, mats, ws_in, bias_in, q_dram, v_dram, out):
    f32, f32r, i32 = mybir.dt.float32, mybir.dt.float32r, mybir.dt.int32
    ALU = mybir.AluOpType
    ACT = mybir.ActivationFunctionType
    X = mybir.AxisListType.X
    ctx = ExitStack()
    with ctx:
        def sb(name, shape, dt=f32, where=ctx):
            return where.enter_context(nc.sbuf_tensor(name, shape, dt))

        def sem(name):
            return ctx.enter_context(nc.semaphore(name))

        x = sb("x", [P, KC, S])
        w_raw = sb("w_raw", [P, 2, KC, P])
        w_hi = sb("w_hi", [P, 2, KC, P], f32r)
        w_lo = sb("w_lo", [P, 2, KC, P], f32r)
        ident = sb("ident", [P, P])
        ones = sb("ones", [P, P])
        colt = sb("colt", [P, cols.shape[1]])
        mod = sb("mod", [P, PARTS, KC])
        amp = sb("amp", [P, 4, KC])
        cond = sb("cond", [P, 3, KC])
        vmean = sb("vmean", [P, KC, 2])
        vscale = sb("vscale", [P, 2, KC])
        root = sb("root", [P, 4 * KC])
        inv = sb("inv", [P, 4 * KC])
        sink8 = sb("sink8", [P, 2 * 4])

        with ExitStack() as first:
            mod_first = sb("mod_first", [P, 2 * KC, S], where=first)
        h_hi = sb("h_hi", [P, KC, S], f32r)
        h_lo = sb("h_lo", [P, KC, S], f32r)

        with ExitStack() as attn:
            kf = sb("kf", [HD, KV, PAD + S], f32, attn)
            vt = sb("vt", [P, PAD + S], f32, attn)
            v_s = sb("v_s", [P, NCH, P], f32, attn)
            with ExitStack() as rope:
                cos = sb("cos", [P, S], f32, rope)
                sin = sb("sin", [P, S], f32, rope)
                qa = sb("qa", [P, 2, S], f32, rope)
                qb = sb("qb", [P, 2, S], f32, rope)
                oa = sb("oa", [P, 2, S], f32, rope)
                ob = sb("ob", [P, 2, S], f32, rope)
            qf = sb("qf", [HD, 2, HALF], f32, attn)
            pr = sb("pr", [P, 2, 4, P + 1], f32, attn)
            pt = sb("pt", [P, 2, HALF], f32, attn)
            v_w = sb("v_w", [P, 2, P], f32, attn)
            small = sb("small", [P, 2, 4, 4], f32, attn)
        with ExitStack() as late:
            mod_late = sb("mod_late", [P, 2 * KC, S], where=late)
        with ExitStack() as gv:
            v_out = sb("v_out", [P, 2, S], f32, gv)
            v_stat = sb("v_stat", [P, KC, VCH, 6], f32, gv)
        hid_hi = sb("hid_hi", [P, KC, S], f32r)
        hid_lo = sb("hid_lo", [P, KC, S], f32r)

        with ExitStack() as gu:
            ws = sb("ws", [P, 4, P], f32, gu)
            bias = sb("bias", [P, 4, P], f32, gu)
            vf = sb("vf", [P, 2, KC, P], f32, gu)
            u_t = sb("u_t", [P, S], f32, gu)
        mod_acc = sb("mod_acc", [P, S])
        tmp = sb("tmp", [P, 2, S])
        mod_t = sb("mod_t", [P, 2, S])
        sumsq = mod_t[:, 1, :]

        pp = [ctx.enter_context(nc.psum_tensor(f"pp{i}", [P, S], f32)) for i in range(4)]

        ngain = lambda n: colt[:, KC * n:KC * n + KC]
        mod_b = lambda part: colt[:, 4 * KC + KC * part:4 * KC + KC * part + KC]
        o = 4 * KC + PARTS * KC
        qgain_a, qgain_b, kgain = (colt[:, o + i:o + i + 1] for i in range(3))
        inv_freq = colt[:, o + 3:o + 4]
        eps = colt[:, o + 4:o + 5]
        vgain0 = o + 5
        sink0 = vgain0 + VCH
        sel_q = colt[:, sink0 + 8:sink0 + 12]
        sel_k = colt[:, sink0 + 12:sink0 + 14]

        raw_in = [sem("raw_in0"), sem("raw_in1")]
        hi_done, lo_done = sem("hi_done"), sem("lo_done")
        gemm = sem("gemm")
        evac = [sem("evac0"), sem("evac1")]
        c_ld, const_in = sem("c_ld"), sem("const_in")
        x_ld = [sem(f"x_ld{i}") for i in range(4)]
        mf_in = [sem(f"mf_in{i}") for i in range(2 * KC)]
        pos_s = sem("pos_s")
        dv = sem("dv")
        cexp, angle, trig = sem("cexp"), sem("angle"), sem("trig")
        mt_in = [sem("mt_in0"), sem("mt_in1")]
        mt_used = sem("mt_used")
        mf_used = sem("mf_used")
        mod_mm, mod_done = sem("mod_mm"), sem("mod_done")
        sq_done, ss_done = sem("sq_done"), sem("ss_done")
        ss_mm, sd_done, rs_done = sem("ss_mm"), sem("sd_done"), sem("rs_done")
        rb_done, bc_done = sem("rb_done"), sem("bc_done")
        t_done, nh_done, h_done = sem("t_done"), sem("nh_done"), sem("h_done")
        q_sq, q_sum, q_ss, q_sd = sem("q_sq"), sem("q_sum"), sem("q_ss"), sem("q_sd")
        q_rc, q_rb, q_bc, q_cs = sem("q_rc"), sem("q_rb"), sem("q_bc"), sem("q_cs")
        k_normed, k_swap, k_roped, kf_in = sem("k_normed"), sem("k_swap"), sem("k_roped"), sem("kf_in")
        q_roped, q_out = sem("q_roped"), sem("q_out")
        pads = sem("pads")
        v_tr, v_cp = sem("v_tr"), sem("v_cp")
        qf_in = [sem("qf_in0"), sem("qf_in1")]
        sc_mm, p_sub, p_exp, p_sum, p_norm = sem("sc_mm"), sem("p_sub"), sem("p_exp"), sem("p_sum"), sem("p_norm")
        p_tr, p_cp, vw, pv_mm, o_hi, o_lo = (sem(n) for n in ("p_tr", "p_cp", "vw", "pv_mm", "o_hi", "o_lo"))
        p_tot, p_max = sem("p_tot"), sem("p_max")
        relu, hd_hi, hid = sem("relu"), sem("hd_hi"), sem("hid")
        vtr_mm, v_stats, v_copied = sem("vtr_mm"), sem("v_stats"), sem("v_copied")
        v_saved = [sem("v_saved0"), sem("v_saved1")]
        v_sd, v_sc, v_aggr, s_gain, ss_zero = sem("v_sd"), sem("v_sc"), sem("v_aggr"), sem("s_gain"), sem("ss_zero")
        vf_in, vn = [sem("vf_in0"), sem("vf_in1")], sem("vn")
        ws_ld, wsz = sem("ws_ld"), sem("wsz")
        sp_mm, t_mul, t_hi = sem("sp_mm"), sem("t_mul"), sem("t_hi")
        late_in = [sem("late_in0"), sem("late_in1")]
        acc_zero = sem("acc_zero")
        sink8_done = sem("sink8_done")
        saved = sem("saved")

        H_N = 2 * KC
        X_WO, X_MLP, X_G = 0, [KC, 7 * KC], 5 * KC
        HID_MLP = [2, 2 + KC * MLP_GROUPS + VCH]
        HID_G = 2 + KC * MLP_GROUPS
        RING_MLP, RING_GV = 2 * KC, 2 * KC + KC * MLP_GROUPS

        def static(*v):
            return all(isinstance(i, int) for i in v)

        block = ctx.enter_context(nc.Block())

        @block.sync
        def _(sp):
            sp.dma_start(cond[:, 0, :], c_in).then_inc(c_ld, 16)
            sp.dma_start(colt[:, :], cols).then_inc(const_in, 16)
            sp.dma_start(ones[:, :], mats[:, 1, :]).then_inc(const_in, 16)
            sp.dma_start(ident[:, :], mats[:, 0, :]).then_inc(const_in, 16)
            sp.dma_start(qa[:, 0, :].bitcast(i32), pos_in).then_inc(pos_s, 16)
            for i in range(4):
                sp.dma_start(x[:, 2 * i:2 * i + 2, :], x_in[:, 2 * i:2 * i + 2, :]).then_inc(x_ld[i], 16)
            for q in range(2 * KC):
                if q == KC:
                    for s in range(2):
                        sp.dma_start(w_raw[:, s, :, :], weights[s]).then_inc(raw_in[s], 16)
                sp.dma_start(mod_first[:, q, :], mod_w[q]).then_inc(mf_in[q], 16)

            def load_block(pair, s):
                sp.wait_ge(lo_done, pair * 2 + (s - 1))
                sp.dma_start(w_raw[:, s, :, :], weights[pair * 2 + s]).then_inc(raw_in[s], 16)

            def save_q(j):
                sp.wait_ge(q_roped, j + 1)
                for i in range(4):
                    head = 4 * (j % 2) + i
                    for part, src in ((0, oa), (1, ob)):
                        sp.dma_start(q_dram[:, j // 2, 32 * part:32 * part + 32, head, :].rearrange("n d t -> d n t"),
                                     src[32 * i:32 * i + 32, (j + 1) % 2, :].rearrange("d (n t) -> d n t", t=CHUNK)).then_inc(q_out, 16)

            with sp.Fori(1, 4) as pair:
                for s in range(2):
                    load_block(pair, s)
            for j in range(3):
                load_block(4 + j, 0)
                save_q(j)
                if j < 2:
                    load_block(4 + j, 1)
            load_block(6, 1)
            save_q(3)

            def load_q(t, n, g):
                if not static(t) or t >= 2:
                    sp.wait_ge(sc_mm, t - 1)
                sp.dma_start(qf[:, g, :], q_dram[n, g]).then_inc(qf_in[g], 16)

            sp.wait_ge(q_out, 16 * 8 * 4)
            for g in range(KV):
                load_q(g, 0, g)
            with sp.Fori(1, NCH) as n:
                for g in range(KV):
                    load_q(n * 2 + g, n, g)

            with sp.Fori(7, UNITS // 2) as pair:
                for s in range(2):
                    load_block(pair, s)

            for n in range(KC):
                sp.wait_ge(evac[n % 2], (UNITS - KC + n) // 2 + 1)
                sp.dma_start(out[n], x[:, n, :]).then_inc(saved, 16)
            sp.wait_ge(saved, 16 * KC)

        @block.gpsimd
        def _(pool):
            def split_lo(pair, s):
                pool.wait_ge(hi_done, pair * 2 + (s + 1))
                nc.gpsimd.tensor_tensor(out=w_lo[:, s, :, :], in0=w_raw[:, s, :, :],
                                        in1=w_hi[:, s, :, :].bitcast(f32), op=ALU.subtract).then_inc(lo_done, 1)

            nc.gpsimd.memset(kf[:, :, 0:PAD], 0.0).then_inc(pads, 1)
            nc.gpsimd.memset(vt[:, 0:PAD], 0.0).then_inc(pads, 1)
            pool.wait_ge(pads, 2)
            with pool.Fori(0, U_WO // 2 + 1) as pair:
                for s in range(2):
                    split_lo(pair, s)

            def normalise(t, g):
                pool.wait_ge(p_sum, t + 1)
                nc.gpsimd.tensor_tensor(out=pr[:, g, :, 0:P], in0=pr[:, g, :, 0:P],
                                        in1=small[:, g, 3, :].unsqueeze(2).to_broadcast([P, 4, P]),
                                        op=ALU.mult).then_inc(p_norm, 1)

            with pool.Fori(0, NCH) as n:
                for g in range(KV):
                    normalise(n * 2 + g, g)

            with pool.Fori(U_WO // 2 + 1, UNITS // 2) as pair:
                for s in range(2):
                    split_lo(pair, s)

        @block.scalar
        def _(act):
            def split_hi(pair, s):
                act.wait_ge(raw_in[s], pair * 16 + 16)
                if not static(pair) or pair:
                    act.wait_ge(gemm, pair * 2 + (s - 1))
                nc.scalar.activation(w_hi[:, s, :, :], w_raw[:, s, :, :], ACT.Copy).then_inc(hi_done, 1)

            def load_mod(q, slot):
                if not static(q) or q >= 2:
                    act.wait_ge(mt_used, q - 1)
                late = 0 if static(q) and q < RING_MLP else 2 * KC
                act.dma_start(mod_t[:, slot, :], mod_w[q + (2 * KC + late)]).then_inc(mt_in[slot], 16)

            def square(k, s):
                nc.scalar.activation(tmp[:, s, :], x[:, bass.ds(k, 1), :].rearrange("p a s -> p (a s)"),
                                     ACT.Square).then_inc(sq_done, 1)

            def norm(n):
                act.wait_ge(ss_mm, n + 1)
                nc.scalar.activation(root[:, 0:KC], pp[2][:, 0:KC], ACT.Sqrt, bias=eps, scale=1.0 / D).then_inc(sd_done, 1)
                act.wait_ge(rs_done, n + 1)
                nc.scalar.activation(tmp[:, 1, :].rearrange("p (b m) -> p b m", m=P),
                                     inv[:, 0:KC].unsqueeze(2).to_broadcast([P, KC, P]), ACT.Copy).then_inc(rb_done, 1)
                act.wait_ge(mod_done, 3 * n + 2)
                with act.Fori(0, KC) as k:
                    for half in range(2):
                        cs = slice(HALF * half, HALF * half + HALF)
                        act.wait_ge(t_done, k * 2 + (H_N * n + half + 1))
                        nc.scalar.activation(h_hi[:, bass.ds(k, 1), cs].rearrange("p a s -> p (a s)"), pp[3][:, cs],
                                             ACT.Identity, bias=mod[:, 3 * n, bass.ds(k, 1)]).then_inc(nh_done, 1)

            act.wait_ge(c_ld, 16)
            nc.scalar.activation(cond[:, 1, :], cond[:, 0, :], ACT.Exp, scale=-1.0).then_inc(cexp, 1)
            for k in range(KC):
                if k % 2 == 0:
                    act.wait_ge(x_ld[k // 2], 16)
                if k >= 2:
                    act.wait_ge(ss_done, k - 1)
                square(k, k % 2)
            act.wait_ge(angle, 1)
            nc.scalar.activation(cos[:, :], cos[:, :], ACT.Sin).then_inc(trig, 1)
            nc.scalar.activation(sin[:, :], sin[:, :], ACT.Sin).then_inc(trig, 1)
            split_hi(0, 0)
            split_hi(0, 1)
            act.wait_ge(const_in, 48)
            norm(0)

            def head_roots(j, heads):
                act.wait_ge(q_ss, j + 2)
                nc.scalar.activation(root[:, 0:heads * KC], pp[2][:, 0:heads * KC], ACT.Sqrt,
                                     bias=eps, scale=1.0 / HD).then_inc(q_sd, 1)
                act.wait_ge(q_rc, j + 2)
                spread = tmp[:, 1, :].rearrange("p (b r h d) -> p b r h d", b=KC, h=heads, d=HD // 2)
                for r in range(4 // heads):
                    ins = nc.scalar.activation(spread[:, :, r, :, :],
                                               inv[:, 0:heads * KC].rearrange("p (b h) -> p b h", h=heads)
                                               .unsqueeze(3).to_broadcast([P, KC, heads, HD // 2]), ACT.Copy)
                ins.then_inc(q_rb, 1)

            load_mod(0, 0)
            load_mod(1, 1)
            act.wait_ge(gemm, U_K + 1)
            split_hi(1, 0)
            nc.scalar.activation(qa[:, 0, :], pp[0][:, :], ACT.Copy).then_inc(evac[0], 1)
            act.wait_ge(evac[0], 1)
            nc.scalar.activation(tmp[:, 0, :], qa[:, 0, :], ACT.Square).then_inc(q_sq, 1)
            act.wait_ge(gemm, U_V + 1)
            split_hi(1, 1)
            nc.scalar.activation(vt[:, PAD:], pp[1][:, :], ACT.Copy).then_inc(evac[1], 1)
            load_mod(2, 0)
            load_mod(3, 1)
            head_roots(-1, KV)
            act.wait_ge(k_normed, 1)
            act.dma_start(qb[0:64, 0, :], qa[64:128, 0, :]).then_inc(k_swap, 16)
            act.dma_start(qb[64:128, 0, :], qa[0:64, 0, :]).then_inc(k_swap, 16)
            load_mod(4, 0)
            load_mod(5, 1)

            for j in range(4):
                pair = U_Q // 2 + j
                slot = (j + 1) % 2
                act.wait_ge(gemm, 2 * pair + 1)
                split_hi(pair + 1, 0)
                if j == 1:
                    act.wait_ge(k_roped, 2)
                elif j:
                    act.wait_ge(q_roped, j - 1)
                nc.scalar.activation(qa[:, slot, :], pp[0][:, :], ACT.Copy).then_inc(evac[0], 1)
                if j:
                    load_mod(5 + 3 * j, (5 + 3 * j) % 2)
                if 6 + 3 * j < 2 * KC:
                    load_mod(6 + 3 * j, j % 2)
                if j == 0:
                    act.wait_ge(k_roped, 2)
                    for g in range(KV):
                        for part in range(2):
                            act.dma_start(kf[32 * part:32 * part + 32, g, PAD:],
                                          oa[64 * part + 32 * g:64 * part + 32 * g + 32, 0, :]).then_inc(kf_in, 16)
                act.wait_ge(gemm, 2 * pair + 2)
                split_hi(pair + 1, 1)
                nc.scalar.activation(qb[:, slot, :], pp[1][:, :], ACT.Copy).then_inc(evac[1], 1)
                if j:
                    act.wait_ge(q_roped, j)
                act.wait_ge(evac[0], 2 + j)
                nc.scalar.activation(tmp[:, 0, :], qa[:, slot, :], ACT.Square).then_inc(q_sq, 1)
                act.wait_ge(evac[1], 2 + j)
                nc.scalar.activation(tmp[:, 1, :], qb[:, slot, :], ACT.Square).then_inc(q_sq, 1)
                if 7 + 3 * j < 2 * KC:
                    load_mod(7 + 3 * j, (7 + 3 * j) % 2)
                act.wait_ge(v_tr, j + 1)
                nc.scalar.activation(v_s[:, 4 * j:4 * j + 4, :],
                                     pp[3][:, 0:HALF].rearrange("p (n c) -> p n c", n=4), ACT.Copy).then_inc(v_cp, 1)
                head_roots(j, 4)

            def probs_copy(t, g):
                act.wait_ge(p_tr, t + 1)
                if not static(t) or t >= 2:
                    act.wait_ge(pv_mm, t - 1)
                nc.scalar.activation(pt[:, g, :], pp[1][:, HALF * g:HALF * g + HALF], ACT.Copy).then_inc(p_cp, 1)

            def out_high(t, n, g):
                act.wait_ge(pv_mm, t + 1)
                rows = slice(64 * g, 64 * g + 64)
                nc.scalar.activation(h_hi[rows, :, bass.ds(n * CHUNK, CHUNK)],
                                     pp[2][rows, HALF * g:HALF * g + HALF].rearrange("p (h t) -> p h t", t=CHUNK),
                                     ACT.Copy).then_inc(o_hi, 1)

            def exps(t, g):
                act.wait_ge(p_sub, t + 1)
                nc.scalar.activation(pr[:, g, :, :], pr[:, g, :, :], ACT.Exp, scale=HD ** -0.5).then_inc(p_exp, 1)

            def window(t, n, e):
                if not static(t) or t >= 4:
                    act.wait_ge(pv_mm, t - 2)
                nc.scalar.activation(v_w[:, e, :], v_s[:, bass.ds(n, 1), :].rearrange("p a c -> p (a c)"),
                                     ACT.Copy).then_inc(vw, 1)

            def step(m, b):
                t = m * 4 + b
                if not static(t) or 2 <= t < 2 * NCH + 2:
                    probs_copy(t - 2, b % 2)
                if not static(t) or 3 <= t:
                    out_high(t - 3, m * 2 + ((b + 1) // 2 - 2), (b + 1) % 2)
                if not static(t) or t < 2 * NCH:
                    exps(t, b % 2)
                    if b % 2 == 0:
                        window(t, m * 2 + b // 2, b // 2)

            act.wait_ge(v_cp, 4)
            for b in range(4):
                step(0, b)
            with act.Fori(1, NCH // 2 - 1) as m:
                for b in range(4):
                    step(m, b)
            for b in range(7):
                step(NCH // 2 - 1 + b // 4, b % 4)

            def residual(pair0, first=0, count=4, split=True):
                with act.Fori(first, first + count) as i:
                    for s in range(2):
                        if split:
                            act.wait_ge(gemm, (i + pair0) * 2 + (s + 1))
                            split_hi(i + (pair0 + 1), s)
                        act.wait_ge(evac[s], i + (pair0 + 1))
                        square(i * 2 + s, s)

            act.wait_ge(o_lo, 2 * NCH)
            for part in range(2):
                act.dma_start(mod_late[:, KC * part:KC * part + KC, :],
                              mod_w[4 * KC + KC * part:4 * KC + KC * part + KC].rearrange("q p s -> p q s")).then_inc(late_in[part], 16)
            residual(U_WO // 2)
            norm(1)

            def mlp(layer):
                pair0 = U_MLP[layer] // 2
                c0 = KC * MLP_GROUPS * layer

                def group(g, last=False):
                    with act.Fori(0, 4) as i:
                        for s in range(2):
                            c = g * KC + i * 2 + s
                            pair = g * 8 + i + pair0
                            if layer == 0:
                                act.wait_ge(ss_done, g * KC + 2 * KC)
                                load_mod(c + RING_MLP, s)
                            act.wait_ge(gemm, pair * 2 + (s + 1))
                            act.wait_ge(hid, c + (HID_MLP[layer] - 1))
                            nc.scalar.activation(tmp[:, s, :], pp[s][:, :], ACT.Relu).then_inc(relu, 1)
                            split_hi(pair + 1, s)
                            act.wait_ge(evac[s], pair + 1)
                            nc.scalar.activation(hid_hi[:, bass.ds(i * 2 + s, 1), :].rearrange("p a s -> p (a s)"),
                                                 tmp[:, s, :], ACT.Copy).then_inc(hd_hi, 1)
                    if last:
                        residual(g * 8 + (pair0 + 4), 0, 3)
                        residual(g * 8 + (pair0 + 4), 3, 1, split=False)
                    else:
                        residual(g * 8 + (pair0 + 4))

                with act.Fori(0, MLP_GROUPS - layer) as g:
                    group(g)
                if layer:
                    group(MLP_GROUPS - 1, last=True)

            mlp(0)
            norm(2)

            def v_unit(i, s):
                c = i * 2 + s
                load_mod(c + RING_GV, s)
                act.wait_ge(gemm, c + (U_GV + 1))
                split_hi(i + (U_GV // 2 + 1), s)
                if not static(c) or c >= 2:
                    act.wait_ge(vtr_mm, c - 1)
                nc.scalar.activation(tmp[:, s, :], pp[s][:, :], ACT.Gelu).then_inc(evac[s], 1)

            def v_copy(c, s, before):
                act.wait_ge(v_stats, c + 1)
                if not static(before) or before:
                    act.wait_ge(v_saved[s], before * 16)
                nc.scalar.activation(v_out[:, s, :], pp[2][:, :], ACT.Copy).then_inc(v_copied, 1)
                act.wait_ge(v_copied, c + 1)
                act.dma_start(v_dram[c], v_out[:, s, :]).then_inc(v_saved[s], 16)

            v_unit(0, 0)
            v_unit(0, 1)
            v_copy(0, 0, 0)
            v_unit(1, 0)
            v_copy(1, 1, 0)
            v_unit(1, 1)
            v_copy(2, 0, 1)
            with act.Fori(2, VCH // 2) as i:
                v_unit(i, 0)
                v_copy(i * 2 - 1, 1, i - 1)
                v_unit(i, 1)
                v_copy(i * 2, 0, i)
            v_copy(VCH - 1, 1, VCH // 2 - 1)
            act.wait_ge(v_aggr, 1)
            nc.scalar.activation(vscale[:, 0, :], vmean[:, :, 1], ACT.Sqrt, bias=eps).then_inc(v_sd, 1)
            for s in range(2):
                act.wait_ge(v_saved[s], 16 * (VCH // 2))

            act.wait_ge(wsz, 1)
            with act.Fori(0, 2) as kb:
                act.wait_ge(ss_done, kb * KC + (2 + MLP_GROUPS) * KC)
                groups = bass.ds(kb * 4, 4)
                act.dma_start(ws[0:64, :, :], ws_in[groups, 0:64, :].rearrange("g j i -> j g i")).then_inc(ws_ld, 16)
                act.dma_start(ws[64:128, :, 64:128],
                              ws_in[groups, 64:128, 64:128].rearrange("g j i -> j g i")).then_inc(ws_ld, 16)
                act.dma_start(bias[:, :, :], bias_in[groups].rearrange("g p i -> p g i")).then_inc(ws_ld, 16)
                with act.Fori(0, 4) as i:
                    for s in range(2):
                        c = kb * KC + i * 2 + s
                        pair = kb * KC + i + U_GU // 2
                        act.wait_ge(hid, c + (HID_G - 1))
                        act.dma_start(vf[:, s, :, :], v_dram[c].rearrange("p (b f) -> p b f", b=KC)).then_inc(vf_in[s], 16)
                        act.wait_ge(gemm, pair * 2 + (s + 1))
                        split_hi(pair + 1, s)
                        act.wait_ge(hid, c + HID_G)
                        nc.scalar.activation(u_t[:, :], pp[s][:, :], ACT.Gelu).then_inc(evac[s], 1)
                        act.wait_ge(t_mul, c + 1)
                        nc.scalar.activation(hid_hi[:, bass.ds(i * 2 + s, 1), :].rearrange("p a s -> p (a s)"),
                                             pp[2][:, :], ACT.Copy).then_inc(t_hi, 1)
                residual(kb * KC + (U_GU // 2 + 4))
            norm(3)
            mlp(1)

        @block.vector
        def _(dve):
            chain = [0]

            def own(ins):
                chain[0] += 1
                ins.then_inc(dv, 1)
                dve.wait_ge(dv, chain[0])

            V = nc.vector

            def add_square(idx, s, first=False):
                dve.wait_ge(sq_done, idx + 1)
                dve.wait_ge(ss_done, idx) if not static(idx) or idx else None
                V.tensor_tensor(out=sumsq, in0=sumsq, in1=tmp[:, s, :], op=ALU.add).then_inc(ss_done, 1)

            def scale_add(tile, k, counter):
                V.scalar_tensor_tensor(out=mod_acc[:, :], in0=tile, scalar=cond[:, 2, bass.ds(k, 1)],
                                       in1=mod_acc[:, :], op0=ALU.mult, op1=ALU.add).then_inc(counter, 1)

            def mod_step(q, k, slot, loads):
                dve.wait_ge(mt_in[slot], loads * 16)
                if not static(q) or q:
                    dve.wait_ge(mt_used, q)
                scale_add(mod_t[:, slot, :], k, mt_used)

            def mod_part(part):
                dve.wait_ge(mod_mm, part + 1)
                V.tensor_tensor(out=mod[:, bass.ds(part, 1), :].rearrange("p a k -> p (a k)"),
                                in0=pp[3][:, HALF:HALF + KC], in1=colt[:, bass.ds(part * KC + 4 * KC, KC)],
                                op=ALU.add).then_inc(mod_done, 1)
                V.memset(mod_acc[:, :], 0.0).then_inc(acc_zero, 1)
                dve.wait_ge(acc_zero, part + 2)

            def deviations(n):
                dve.wait_ge(sd_done, n + 1)
                V.reciprocal(inv[:, 0:KC], root[:, 0:KC]).then_inc(rs_done, 1)

            def norm(n):
                dve.wait_ge(mod_done, 3 * n + 2)
                own(V.scalar_tensor_tensor(out=amp[:, n, :], in0=mod[:, 3 * n + 1, :], scalar=1.0,
                                           in1=colt[:, KC * n:KC * n + KC], op0=ALU.add, op1=ALU.mult))
                dve.wait_ge(bc_done, n + 1)

                def scaled(k, half):
                    cs = slice(HALF * half, HALF * half + HALF)
                    V.scalar_tensor_tensor(out=pp[3][:, cs], in0=x[:, bass.ds(k, 1), cs].rearrange("p a s -> p (a s)"),
                                           scalar=amp[:, n, bass.ds(k, 1)], in1=pp[2][:, cs],
                                           op0=ALU.mult, op1=ALU.mult).then_inc(t_done, 1)

                def low(k, half):
                    cs = slice(HALF * half, HALF * half + HALF)
                    dve.wait_ge(nh_done, k * 2 + (H_N * n + half + 1))
                    V.scalar_tensor_tensor(out=h_lo[:, bass.ds(k, 1), cs].rearrange("p a s -> p (a s)"),
                                           in0=pp[3][:, cs], scalar=mod[:, 3 * n, bass.ds(k, 1)],
                                           in1=h_hi[:, bass.ds(k, 1), cs].rearrange("p a s -> p (a s)").bitcast(f32),
                                           op0=ALU.add, op1=ALU.subtract).then_inc(h_done, 1)

                scaled(0, 0)
                scaled(0, 1)
                with dve.Fori(0, KC - 1) as k:
                    for half in range(2):
                        low(k, half)
                        dve.wait_ge(h_done, k * 2 + (H_N * n + half + 1))
                        scaled(k + 1, half)
                low(KC - 1, 0)
                low(KC - 1, 1)

            V.memset(vscale[:, 0, :], 0.0).then_inc(hid, 1)
            V.memset(vscale[:, 1, :], 0.0).then_inc(hid, 1)
            own(V.memset(sumsq, 0.0))
            V.memset(mod_acc[:, :], 0.0).then_inc(acc_zero, 1)
            dve.wait_ge(cexp, 1)
            own(V.tensor_scalar(cond[:, 1, :], cond[:, 1, :], 1.0, None, ALU.add))
            own(V.reciprocal(cond[:, 1, :], cond[:, 1, :]))
            own(V.tensor_tensor(out=cond[:, 2, :], in0=cond[:, 0, :], in1=cond[:, 1, :], op=ALU.mult))
            dve.wait_ge(pos_s, 16)
            dve.wait_ge(const_in, 48)
            V.tensor_scalar(sink8[:, :], colt[:, sink0:sink0 + 2 * 4], 8.0, None, ALU.mult).then_inc(sink8_done, 1)
            own(V.tensor_copy(cos[:, :], qa[:, 0, :].bitcast(i32)))
            own(V.tensor_scalar(sin[:, :], cos[:, :], inv_freq, None, ALU.mult))
            own(V.tensor_scalar(cos[:, :], sin[:, :], 1.0 / TWO_PI, MAGIC, ALU.mult, ALU.add))
            own(V.tensor_scalar(cos[:, :], cos[:, :], MAGIC, None, ALU.subtract))
            for part in (TWO_PI_1, TWO_PI_2, TWO_PI_3):
                own(V.scalar_tensor_tensor(out=sin[:, :], in0=cos[:, :], scalar=-part, in1=sin[:, :],
                                           op0=ALU.mult, op1=ALU.add))
            own(V.tensor_scalar(sin[:, :], sin[:, :], -PI, PI, ALU.max, ALU.min))
            own(V.scalar_tensor_tensor(out=cos[:, :], in0=sin[:, :], scalar=-1.0, in1=sin[:, :],
                                       op0=ALU.mult, op1=ALU.max))
            V.tensor_scalar(cos[:, :], cos[:, :], -1.0, PI / 2, ALU.mult, ALU.add).then_inc(angle, 1)
            for k in range(KC):
                add_square(k, k % 2)
            deviations(0)
            for part in range(2):
                dve.wait_ge(acc_zero, part + 1)
                for k in range(KC):
                    q = part * KC + k
                    dve.wait_ge(mf_in[q], 16)
                    if q:
                        dve.wait_ge(mf_used, q)
                    scale_add(mod_first[:, q, :], k, mf_used)
                mod_part(part)
            norm(0)

            dve.wait_ge(trig, 2)
            mod_q = [0]

            def mods(count):
                for _ in range(count):
                    q = mod_q[0]
                    mod_step(q, q % KC, q % 2, q // 2 + 1)
                    mod_q[0] += 1

            def head_reciprocals(j, heads):
                dve.wait_ge(q_sd, j + 2)
                V.reciprocal(inv[:, 0:heads * KC], root[:, 0:heads * KC]).then_inc(q_rc, 1)
                dve.wait_ge(q_bc, j + 2)

            mods(2)
            head_reciprocals(-1, KV)
            V.scalar_tensor_tensor(out=qa[:, 0, :], in0=qa[:, 0, :], scalar=kgain, in1=pp[2][:, :],
                                   op0=ALU.mult, op1=ALU.mult).then_inc(k_normed, 1)
            mods(2)
            dve.wait_ge(k_normed, 1)
            own(V.tensor_tensor(out=tmp[:, 0, :], in0=qa[:, 0, :], in1=cos[:, :], op=ALU.mult))
            dve.wait_ge(k_swap, 32)
            own(V.tensor_tensor(out=tmp[:, 1, :], in0=qb[:, 0, :], in1=sin[:, :], op=ALU.mult))
            for r, op in ((slice(0, 64), ALU.subtract), (slice(64, 128), ALU.add)):
                V.tensor_tensor(out=oa[r, 0, :], in0=tmp[r, 0, :], in1=tmp[r, 1, :], op=op).then_inc(k_roped, 1)
            for j in range(4):
                slot = (j + 1) % 2
                mods(1)
                dve.wait_ge(q_sq, 1 + 2 * (j + 1))
                V.tensor_tensor(out=tmp[:, 0, :], in0=tmp[:, 0, :], in1=tmp[:, 1, :], op=ALU.add).then_inc(q_sum, 1)
                if j == 1:
                    mod_part(2)
                mods(1)
                head_reciprocals(j, 4)
                V.tensor_tensor(out=tmp[:, 0, :], in0=cos[:, :], in1=pp[2][:, :], op=ALU.mult).then_inc(q_cs, 1)
                V.tensor_tensor(out=tmp[:, 1, :], in0=sin[:, :], in1=pp[2][:, :], op=ALU.mult).then_inc(q_cs, 1)
                dve.wait_ge(q_cs, 2 * j + 2)
                if j == 1:
                    dve.wait_ge(kf_in, 16 * 4)
                elif j:
                    dve.wait_ge(q_out, 16 * 8 * (j - 1))

                def turn(dst, src, gain, by):
                    own(V.scalar_tensor_tensor(out=dst[:, slot, :], in0=src[:, slot, :], scalar=gain, in1=tmp[:, by, :],
                                               op0=ALU.mult, op1=ALU.mult))

                turn(oa, qa, qgain_a, 0)
                turn(ob, qb, qgain_b, 1)
                own(V.tensor_tensor(out=oa[:, slot, :], in0=oa[:, slot, :], in1=ob[:, slot, :], op=ALU.subtract))
                turn(qb, qb, qgain_b, 0)
                turn(qa, qa, qgain_a, 1)
                V.tensor_tensor(out=ob[:, slot, :], in0=qb[:, slot, :], in1=qa[:, slot, :], op=ALU.add).then_inc(q_roped, 1)
                mods(1)
            mod_part(3)

            def sums(t, g):
                dve.wait_ge(p_exp, t + 1)
                if not static(t) or t >= 2:
                    dve.wait_ge(p_norm, t - 1)
                V.tensor_reduce(out=small[:, g, 2, :], in_=pr[:, g, :, :], axis=X, op=ALU.add).then_inc(p_tot, 1)
                dve.wait_ge(p_tot, t + 1)
                V.reciprocal(small[:, g, 3, :], small[:, g, 2, :]).then_inc(p_sum, 1)

            def maxima(t, g):
                lo = PAD if static(t) and t < 2 else 0
                sc = pp[0][:, HALF * g:HALF * g + HALF].rearrange("p (r k) -> p r k", k=P)
                dve.wait_ge(sc_mm, t + 1)
                if not static(t) or t >= 2:
                    dve.wait_ge(p_tr, t - 1)
                V.tensor_reduce(out=small[:, g, 0, :], in_=sc[:, :, lo:], axis=X, op=ALU.max).then_inc(p_max, 1)
                dve.wait_ge(p_max, t * 2 + 1)
                V.tensor_tensor(out=small[:, g, 1, :], in0=small[:, g, 0, :], in1=sink8[:, 4 * g:4 * g + 4],
                                op=ALU.max).then_inc(p_max, 1)
                dve.wait_ge(p_max, t * 2 + 2)
                if lo:
                    V.memset(pr[:, g, :, 0:lo], -1.0e4)
                V.tensor_tensor(out=pr[:, g, :, P:P + 1], in0=sink8[:, 4 * g:4 * g + 4].unsqueeze(2),
                                in1=small[:, g, 1, :].unsqueeze(2), op=ALU.subtract)
                V.tensor_tensor(out=pr[:, g, :, lo:P], in0=sc[:, :, lo:],
                                in1=small[:, g, 1, :].unsqueeze(2).to_broadcast([P, 4, P - lo]),
                                op=ALU.subtract).then_inc(p_sub, 1)

            def out_low(t, n, g):
                rows = slice(64 * g, 64 * g + 64)
                cs = bass.ds(n * CHUNK, CHUNK)
                dve.wait_ge(o_hi, t + 1)
                V.tensor_tensor(out=h_lo[rows, :, cs],
                                in0=pp[2][rows, HALF * g:HALF * g + HALF].rearrange("p (h t) -> p h t", t=CHUNK),
                                in1=h_hi[rows, :, cs].bitcast(f32), op=ALU.subtract).then_inc(o_lo, 1)

            def step(m, b):
                t = m * 4 + b
                if not static(t) or 1 <= t < 2 * NCH + 1:
                    sums(t - 1, (b + 1) % 2)
                if not static(t) or t < 2 * NCH:
                    maxima(t, b % 2)
                if not static(t) or 3 <= t:
                    out_low(t - 3, m * 2 + ((b + 1) // 2 - 2), (b + 1) % 2)

            dve.wait_ge(sink8_done, 1)
            for b in range(4):
                step(0, b)
            with dve.Fori(1, NCH // 2 - 1) as m:
                for b in range(4):
                    step(m, b)
            for b in range(7):
                step(NCH // 2 - 1 + b // 4, b % 4)

            def residual(pair0, n0, gate, first=0, count=4, late=None, zeroed=None):
                with dve.Fori(first, first + count) as i:
                    for s in range(2):
                        xn = x[:, bass.ds(i * 2 + s, 1), :].rearrange("p a s -> p (a s)")
                        dve.wait_ge(gemm, (i + pair0) * 2 + (s + 1))
                        V.scalar_tensor_tensor(out=xn, in0=pp[s][:, :], scalar=mod[:, gate, bass.ds(i * 2 + s, 1)],
                                               in1=xn, op0=ALU.mult, op1=ALU.add).then_inc(evac[s], 1)
                        if zeroed is not None:
                            dve.wait_ge(ss_zero, zeroed)
                        if late is not None:
                            for r in range(2):
                                k = (i - first) * 4 + (2 * s + r)
                                dve.wait_ge(mf_used, k + (2 * KC + KC * late))
                                scale_add(mod_late[:, bass.ds(k + KC * late, 1), :].rearrange("p a s -> p (a s)"), k, mf_used)
                        add_square(i * 2 + (n0 + KC + s), s)

            own(V.memset(sumsq, 0.0))
            for late in range(2):
                dve.wait_ge(late_in[late], 16)
                residual(U_WO // 2, X_WO, GATE1, 2 * late, 2, late)
                mod_part(4 + late)
            deviations(1)
            norm(1)

            def mlp(layer):
                pair0 = U_MLP[layer] // 2
                c0 = KC * MLP_GROUPS * layer
                with dve.Fori(0, MLP_GROUPS) as g:
                    with dve.Fori(0, 4) as i:
                        for s in range(2):
                            c = g * KC + i * 2 + s
                            if layer == 0:
                                mod_step(c + RING_MLP, i * 2 + s, s, g * 4 + i + (RING_MLP // 2 + 1))
                            dve.wait_ge(relu, c + (c0 + 1))
                            V.scalar_tensor_tensor(out=tmp[:, s, :], in0=pp[s][:, :], scalar=0.0, in1=tmp[:, s, :],
                                                   op0=ALU.max, op1=ALU.mult).then_inc(evac[s], 1)
                            dve.wait_ge(hd_hi, c + (c0 + 1))
                            V.tensor_tensor(out=hid_lo[:, bass.ds(i * 2 + s, 1), :].rearrange("p a s -> p (a s)"),
                                            in0=tmp[:, s, :],
                                            in1=hid_hi[:, bass.ds(i * 2 + s, 1), :].rearrange("p a s -> p (a s)").bitcast(f32),
                                            op=ALU.subtract).then_inc(hid, 1)
                    if layer == 0:
                        mod_part(g + 6)
                    V.memset(sumsq, 0.0).then_inc(ss_zero, 1)
                    residual(g * 8 + (pair0 + 4), g * KC + X_MLP[layer], 6 * layer + GATE2,
                             zeroed=g + (1 + layer * (MLP_GROUPS + 2)))

            mlp(0)
            deviations(2)
            norm(2)

            for half in range(2):
                with dve.Fori(4 * half, 4 * half + 4) as i:
                    for s in range(2):
                        c = i * 2 + s
                        mod_step(c + RING_GV, c - KC * half, s, i + (RING_GV // 2 + 1))
                        dve.wait_ge(vtr_mm, c + 1)
                        for b in range(KC):
                            ins = V.bn_stats(v_stat[:, b, bass.ds(c, 1), :].rearrange("p a s -> p (a s)"),
                                             pp[2][:, P * b:P * b + P])
                        ins.then_inc(v_stats, 1)
                mod_part(10 + half)
            dve.wait_ge(v_stats, VCH)
            for b in range(KC):
                ins = V.bn_aggr(vmean[:, b, :], v_stat[:, b, :, :].rearrange("p c s -> p (c s)"))
            ins.then_inc(v_aggr, 1)
            dve.wait_ge(v_sd, 1)
            own(V.reciprocal(vscale[:, 0, :], vscale[:, 0, :]))
            V.scalar_tensor_tensor(out=vscale[:, 1, :], in0=vmean[:, :, 0], scalar=-1.0, in1=vscale[:, 0, :],
                                   op0=ALU.mult, op1=ALU.mult).then_inc(v_sc, 1)
            dve.wait_ge(v_sc, 1)
            V.memset(ws[64:128, :, 0:64], 0.0).then_inc(wsz, 1)

            with dve.Fori(0, 2) as kb:
                with dve.Fori(0, 4) as i:
                    for s in range(2):
                        c = kb * KC + i * 2 + s
                        pair = kb * KC + i + U_GU // 2
                        dve.wait_ge(vf_in[s], kb * 64 + i * 16 + 16)
                        for b in range(KC):
                            ins = V.tensor_scalar(vf[:, s, b, :], vf[:, s, b, :], vscale[:, 0, b:b + 1],
                                                  vscale[:, 1, b:b + 1], ALU.mult, ALU.add)
                        ins.then_inc(vn, 1)
                        mixed = pp[2][:, :].rearrange("p (b t) -> p b t", b=KC)
                        dve.wait_ge(sp_mm, c + 1)
                        V.scalar_tensor_tensor(out=mixed, in0=mixed, scalar=colt[:, bass.ds(c + vgain0, 1)],
                                               in1=bias[:, bass.ds(i, 1), :].to_broadcast([P, KC, P]),
                                               op0=ALU.mult, op1=ALU.add).then_inc(s_gain, 1)
                        dve.wait_ge(s_gain, c + 1)
                        dve.wait_ge(evac[s], pair + 1)
                        V.tensor_tensor(out=pp[2][:, :], in0=pp[2][:, :], in1=u_t[:, :], op=ALU.mult).then_inc(t_mul, 1)
                        dve.wait_ge(t_hi, c + 1)
                        V.tensor_tensor(out=hid_lo[:, bass.ds(i * 2 + s, 1), :].rearrange("p a s -> p (a s)"),
                                        in0=pp[2][:, :],
                                        in1=hid_hi[:, bass.ds(i * 2 + s, 1), :].rearrange("p a s -> p (a s)").bitcast(f32),
                                        op=ALU.subtract).then_inc(hid, 1)
                V.memset(sumsq, 0.0).then_inc(ss_zero, 1)
                residual(kb * KC + (U_GU // 2 + 4), kb * KC + X_G, 6 + GATE1, zeroed=kb + (MLP_GROUPS + 1))
            deviations(3)
            norm(3)
            mlp(1)

        @block.tensor
        def _(pe):
            T = nc.tensor

            def ready(pair, s):
                pe.wait_ge(lo_done, pair * 2 + (s + 1))
                if not static(pair) or pair:
                    pe.wait_ge(evac[s], pair)

            def products(s, k, hi, lo):
                for w, parts in ((w_hi, (hi, lo)), (w_lo, (hi,))):
                    for r in parts:
                        for half in range(2):
                            cs = slice(HALF * half, HALF * half + HALF)
                            last = T.matmul(pp[s][:, cs], w[:, s, k, :], r[:, k, cs],
                                            start=(k == 0 and w is w_hi and r is hi),
                                            stop=(k == KC - 1 and w is w_lo))
                return last

            def unit(pair, s, hi, lo, chunk_ready=None, hooks=None):
                ready(pair, s)
                for k in range(KC):
                    if chunk_ready:
                        pe.wait_ge(chunk_ready[0], chunk_ready[1] + k)
                    last = products(s, k, hi, lo)
                    if hooks and k in hooks:
                        hooks[k]()
                last.then_inc(gemm, 1)

            def normed_pair(pair, n):
                ready(pair, 0)
                ready(pair, 1)
                for k in range(KC + LAG):
                    if k < KC:
                        pe.wait_ge(h_done, H_N * n + 2 * k + 2)
                        last = products(0, k, h_hi, h_lo)
                        if k == KC - 1:
                            last.then_inc(gemm, 1)
                    if k >= LAG:
                        last = products(1, k - LAG, h_hi, h_lo)
                last.then_inc(gemm, 1)

            def mod_columns(part, counter, count):
                pe.wait_ge(counter, count)
                for k in range(KC):
                    last = T.matmul(pp[3][:, HALF + k:HALF + k + 1], mod_acc[:, P * k:P * k + P], ones[:, 0:1],
                                    start=True, stop=True)
                last.then_inc(mod_mm, 1)

            def token_sums(heads, select, counter):
                src = mod_t[:, 1, :] if select is None else tmp[:, 0, :]
                sel = ones[:, 0:1] if select is None else select
                for b in range(KC):
                    last = T.matmul(pp[2][:, heads * b:heads * b + heads], src[:, P * b:P * b + P], sel,
                                    start=True, stop=True)
                last.then_inc(counter, 1)

            def spread(counter):
                for b in range(KC):
                    last = T.matmul(pp[2][:, P * b:P * b + P], tmp[:, 1, P * b:P * b + P], ident[:, :],
                                    start=True, stop=True)
                last.then_inc(counter, 1)

            def sum_squares(n, squares):
                pe.wait_ge(ss_done, squares)
                token_sums(1, None, ss_mm)
                pe.wait_ge(rb_done, n + 1)
                spread(bc_done)

            pe.wait_ge(const_in, 48)
            sum_squares(0, KC)
            for part in range(2):
                mod_columns(part, mf_used, KC * part + KC)

            def head_squares(j):
                if j < 0:
                    pe.wait_ge(q_sq, 1)
                else:
                    pe.wait_ge(q_sum, j + 1)
                    if j:
                        pe.wait_ge(q_cs, 2 * j)
                    else:
                        pe.wait_ge(k_normed, 1)
                token_sums(*((KV, sel_k) if j < 0 else (4, sel_q)), q_ss)

            def head_spread(j):
                pe.wait_ge(q_rb, j + 2)
                spread(q_bc)

            normed_pair(0, 0)
            for j in range(4):
                unit(1 + j, 0, h_hi, h_lo, hooks={3: lambda: head_squares(j - 1), 6: lambda: head_spread(j - 1)})
                unit(1 + j, 1, h_hi, h_lo)
                if j == 1:
                    mod_columns(2, mt_used, KC)
                pe.wait_ge(evac[1], 1)
                pe.wait_ge(pads, 2)
                if j:
                    pe.wait_ge(v_cp, j)
                for r in range(4):
                    n = 4 * j + r
                    last = T.transpose(pp[3][:, P * r:P * r + P], vt[:, CHUNK * n:CHUNK * n + P], ident[:, :])
                last.then_inc(v_tr, 1)
            head_squares(3)
            head_spread(3)
            mod_columns(3, mt_used, 2 * KC)

            def scores(t, n, g):
                pe.wait_ge(qf_in[g], n * 16 + 16)
                if not static(t) or t >= 2:
                    pe.wait_ge(p_sub, t - 1)
                for r in range(4):
                    last = T.matmul(pp[0][:, HALF * g + P * r:HALF * g + P * r + P], qf[:, g, P * r:P * r + P],
                                    kf[:, g, bass.ds(n * CHUNK, P)], start=True, stop=True)
                last.then_inc(sc_mm, 1)

            def turn(t, g):
                pe.wait_ge(p_norm, t + 1)
                if not static(t) or t >= 2:
                    pe.wait_ge(p_cp, t - 1)
                for r in range(4):
                    last = T.transpose(pp[1][:, HALF * g + P * r:HALF * g + P * r + P], pr[:, g, r, 0:P], ident[:, :])
                last.then_inc(p_tr, 1)

            def mix(t, n, g, e):
                pe.wait_ge(p_cp, t + 1)
                pe.wait_ge(vw, n + 1)
                if not static(t) or t >= 2:
                    pe.wait_ge(o_lo, t - 1)
                T.matmul(pp[2][:, HALF * g:HALF * g + HALF], v_w[:, e, :], pt[:, g, :],
                         start=True, stop=True).then_inc(pv_mm, 1)

            def step(m, b):
                t = m * 4 + b
                if not static(t) or t + 1 < 2 * NCH:
                    scores(t + 1, m * 2 + (b + 1) // 2, (b + 1) % 2)
                if not static(t) or 2 <= t < 2 * NCH + 2:
                    mix(t - 2, m * 2 + (b // 2 - 1), b % 2, (b // 2 + 1) % 2)
                if not static(t) or 1 <= t < 2 * NCH + 1:
                    turn(t - 1, (b + 1) % 2)

            pe.wait_ge(kf_in, 16 * 4)
            pe.wait_ge(evac[0], U_WO // 2)
            pe.wait_ge(evac[1], U_WO // 2)
            pe.wait_ge(q_cs, 8)
            scores(0, 0, 0)
            for b in range(4):
                step(0, b)
            with pe.Fori(1, NCH // 2 - 1) as m:
                for b in range(4):
                    step(m, b)
            for b in range(6):
                step(NCH // 2 - 1 + b // 4, b % 4)

            pe.wait_ge(o_lo, 2 * NCH)
            for late in range(2):
                with pe.Fori(U_WO // 2 + 2 * late, U_WO // 2 + 2 * late + 2) as pair:
                    for s in range(2):
                        unit(pair, s, h_hi, h_lo)
                mod_columns(4 + late, mf_used, 3 * KC + KC * late)
            sum_squares(1, 2 * KC)

            def h_units(pair0, first, count=4):
                with pe.Fori(first, count) as i:
                    for s in range(2):
                        unit(i + pair0, s, h_hi, h_lo)

            def hid_units(pair0, hid0, after=None):
                unit(pair0, 0, hid_hi, hid_lo, (hid, hid0 + 1))
                if after:
                    after()
                unit(pair0, 1, hid_hi, hid_lo)
                with pe.Fori(1, 4) as i:
                    for s in range(2):
                        unit(i + pair0, s, hid_hi, hid_lo)

            def mlp(layer):
                pair0 = U_MLP[layer] // 2
                normed_pair(pair0, 2 * layer + 1)
                h_units(pair0, 1)

                def down(g):
                    columns = (lambda: mod_columns(g + 6, mt_used, g * KC + (RING_MLP + KC))) if layer == 0 else None
                    hid_units(g * 8 + (pair0 + 4), g * KC + HID_MLP[layer], columns)

                down(0)
                with pe.Fori(1, MLP_GROUPS) as g:
                    h_units(g * 8 + pair0, 0)
                    down(g)

            mlp(0)
            sum_squares(2, (2 + MLP_GROUPS) * KC)

            def v_turn(c, s, pair):
                pe.wait_ge(evac[s], pair + 1)
                if not static(c) or c:
                    pe.wait_ge(v_copied, c)
                for b in range(KC):
                    last = T.transpose(pp[2][:, P * b:P * b + P], tmp[:, s, P * b:P * b + P], ident[:, :])
                last.then_inc(vtr_mm, 1)

            gv = U_GV // 2
            normed_pair(gv, 2)
            v_turn(0, 0, gv)
            with pe.Fori(1, 4) as i:
                unit(i + gv, 0, h_hi, h_lo)
                v_turn(i * 2 - 1, 1, i + (gv - 1))
                unit(i + gv, 1, h_hi, h_lo)
                v_turn(i * 2, 0, i + gv)
            unit(gv + 4, 0, h_hi, h_lo)
            v_turn(7, 1, gv + 3)
            mod_columns(10, mt_used, RING_GV + KC)
            unit(gv + 4, 1, h_hi, h_lo)
            v_turn(8, 0, gv + 4)
            with pe.Fori(5, 8) as i:
                unit(i + gv, 0, h_hi, h_lo)
                v_turn(i * 2 - 1, 1, i + (gv - 1))
                unit(i + gv, 1, h_hi, h_lo)
                v_turn(i * 2, 0, i + gv)
            v_turn(VCH - 1, 1, gv + 7)
            mod_columns(11, mt_used, RING_GV + 2 * KC)

            def blend(c, s, kb, i):
                pe.wait_ge(vn, c + 1)
                pe.wait_ge(ws_ld, kb * 48 + 48)
                pe.wait_ge(hid, c + HID_G)
                for b in range(KC):
                    last = T.matmul(pp[2][:, P * b:P * b + P], vf[:, s, b, :],
                                    ws[:, bass.ds(i, 1), :].rearrange("p a t -> p (a t)"), start=True, stop=True)
                last.then_inc(sp_mm, 1)

            with pe.Fori(0, 2) as kb:
                with pe.Fori(0, 4) as i:
                    for s in range(2):
                        unit(kb * KC + i + U_GU // 2, s, h_hi, h_lo)
                        blend(kb * KC + i * 2 + s, s, kb, i)
                hid_units(kb * KC + (U_GU // 2 + 4), kb * KC + HID_G)
            sum_squares(3, (4 + MLP_GROUPS) * KC)
            mlp(1)


def kernel(x, c, positions, norm1_gain, norm2_gain, mod_w, mod_b, swa_w_qkv, swa_q_gain, swa_k_gain,
           swa_sinks, swa_w_o, gmlp_w_uv, gmlp_v_gain, gmlp_w_s, gmlp_s_bias, gmlp_w_o, sb_w_qkv, sb_w_o,
           mlp_w1, mlp_w2):
    import numpy as np
    import concourse.bacc as bacc
    from concourse.bass_utils import run_bass_kernel_spmd

    def blocks(w):
        k, n = w.shape
        return w.reshape(k // D, KC, P, n // P, P).transpose(0, 3, 2, 1, 4)

    def columns(v):
        return v.reshape(-1, P).T

    f = {k: np.asarray(v) for k, v in dict(
        x=x, c=c, positions=positions, n1=norm1_gain, n2=norm2_gain, mw=mod_w, mb=mod_b, qkv=swa_w_qkv, qg=swa_q_gain,
        kg=swa_k_gain, sinks=swa_sinks, wo=swa_w_o, uv=gmlp_w_uv, vg=gmlp_v_gain, ws=gmlp_w_s, sb=gmlp_s_bias,
        go=gmlp_w_o, w1=mlp_w1, w2=mlp_w2).items()}
    wq = f["qkv"][0][:, :HEADS * HD].reshape(D, 4, 4, 2, HD // 2).transpose(0, 1, 3, 2, 4).reshape(D, HEADS * HD)
    wk = f["qkv"][0][:, HEADS * HD:HEADS * HD + P].reshape(D, KV, 2, HD // 2).transpose(0, 2, 1, 3).reshape(D, P)
    wv = f["qkv"][0][:, HEADS * HD + P:]
    wo = f["wo"][0].reshape(KV, GROUP, HD, D).transpose(1, 0, 2, 3).reshape(D, D)
    order = [blocks(wk)[0], blocks(wv)[0], blocks(wq)[0], blocks(wo)[0]]

    def mlp_blocks(layer):
        up, down = blocks(f["w1"][layer])[0], blocks(f["w2"][layer])
        for g in range(MLP_GROUPS):
            order.extend((up[KC * g:KC * g + KC], down[g]))

    mlp_blocks(0)
    uv, go = blocks(f["uv"][0])[0], blocks(f["go"][0])
    order.append(uv[VCH:])
    for kb in range(2):
        order.extend((uv[KC * kb:KC * kb + KC], go[kb]))
    mlp_blocks(1)

    half = np.concatenate([f["qg"][0][:HD // 2]] * 4), np.concatenate([f["qg"][0][HD // 2:]] * 4)
    kgain = np.concatenate([f["kg"][0][:HD // 2]] * 2 + [f["kg"][0][HD // 2:]] * 2)
    freq = (10000.0 ** (-np.arange(0, HD, 2) / HD)).astype(np.float32)
    sinks = np.repeat(f["sinks"][0].reshape(KV * 4, 2).T, CHUNK, axis=0)
    cols = np.concatenate(
        [columns(g) for g in (f["n1"][0], f["n2"][0], f["n1"][1], f["n2"][1])]
        + [columns(f["mb"].reshape(-1))]
        + [a[:, None] for a in (half[0], half[1], kgain, np.tile(freq, 4), np.full(P, EPS, np.float32))]
        + [columns(f["vg"][0]), sinks, (np.arange(P)[:, None] // 32 == np.arange(4)).astype(np.float32),
           (np.arange(P)[:, None] // 32 % 2 == np.arange(KV)).astype(np.float32)], axis=1)
    mats = np.stack([np.eye(P), np.ones((P, P))], axis=1).astype(np.float32)
    arrays = {
        "x_in": f["x"][0].T.reshape(KC, P, S).transpose(1, 0, 2),
        "c_in": columns(f["c"][0]),
        "pos_in": np.broadcast_to(f["positions"][0], (P, S)),
        "weights": np.concatenate(order),
        "mod_w": f["mw"].reshape(2, KC, P, 6, D).transpose(0, 3, 1, 2, 4).reshape(PARTS * KC, P, D),
        "cols": cols,
        "mats": mats,
        "ws_in": f["ws"][0].transpose(0, 2, 1),
        "bias_in": np.broadcast_to(f["sb"][0][:, None, :], (KC, P, P)),
    }
    arrays = {k: np.ascontiguousarray(v) for k, v in arrays.items()}
    nc = bacc.Bacc("TRN2", target_bir_lowering=False, num_devices=1)
    dram = {k: nc.dram_tensor(k, a.shape, mybir.dt.from_np(a.dtype), kind="ExternalInput").ap() for k, a in arrays.items()}
    q_dram = nc.dram_tensor("q_dram", (NCH, KV, HD, GROUP, CHUNK), mybir.dt.float32, kind="Internal").ap()
    v_dram = nc.dram_tensor("v_dram", (VCH, P, S), mybir.dt.float32, kind="Internal").ap()
    out = nc.dram_tensor("out", (KC, P, S), mybir.dt.float32, kind="ExternalOutput").ap()
    build(nc, q_dram=q_dram, v_dram=v_dram, out=out, **dram)
    got = run_bass_kernel_spmd(nc, [arrays], core_ids=[0]).results[0]["out"]
    return np.ascontiguousarray(got.reshape(D, S).T)[None]
```

```python
import concourse.bass as bass
from concourse import mybir
from contextlib import ExitStack

D = 1024
S = 1024
P = 128
KC = D // P
HALF = 512
HEADS, KV, HD = 16, 2, 64
GROUP = HEADS // KV
CHUNK = 64
NCH = S // CHUNK
PAD = CHUNK
HIDDEN = 4 * D
MLP_GROUPS = HIDDEN // D
GWIDTH = 2 * D
VCH = GWIDTH // P
EPS = 1e-6
MAGIC = 12582912.0
TWO_PI_1 = 6.28125
TWO_PI_2 = 0.0019350051879882812
TWO_PI_3 = 3.019915981956753e-07
PI = 3.1415925
TWO_PI = 6.283185307179586
LAG = 3

U_Q, U_K, U_V = 0, KC, KC + 1
U_WO = KC + 2
U_MLP = [U_WO + KC, 0]
U_GV = U_MLP[0] + 2 * KC * MLP_GROUPS
U_GU = U_GV + VCH
U_MLP[1] = U_GU + 2 * 2 * KC
UNITS = U_MLP[1] + 2 * KC * MLP_GROUPS
SHIFT1, SCALE1, GATE1, SHIFT2, SCALE2, GATE2 = range(6)
PARTS = 12


def build(nc, x_in, c_in, pos_in, weights, mod_w, cols, mats, ws_in, bias_in, q_dram, v_dram, out):
    f32, f32r, i32 = mybir.dt.float32, mybir.dt.float32r, mybir.dt.int32
    ALU = mybir.AluOpType
    ACT = mybir.ActivationFunctionType
    X = mybir.AxisListType.X
    ctx = ExitStack()
    with ctx:
        def sb(name, shape, dt=f32, where=ctx):
            return where.enter_context(nc.sbuf_tensor(name, shape, dt))

        def sem(name):
            return ctx.enter_context(nc.semaphore(name))

        x = sb("x", [P, KC, S])
        w_raw = sb("w_raw", [P, 2, KC, P])
        w_hi = sb("w_hi", [P, 2, KC, P], f32r)
        w_lo = sb("w_lo", [P, 2, KC, P], f32r)
        ident = sb("ident", [P, P])
        ones = sb("ones", [P, P])
        colt = sb("colt", [P, cols.shape[1]])
        mod = sb("mod", [P, PARTS, KC])
        amp = sb("amp", [P, 4, KC])
        cond = sb("cond", [P, 3, KC])
        vmean = sb("vmean", [P, KC, 2])
        vscale = sb("vscale", [P, 2, KC])
        root = sb("root", [P, 4 * KC])
        inv = sb("inv", [P, 4 * KC])
        sink8 = sb("sink8", [P, 2 * 4])

        with ExitStack() as first:
            mod_first = sb("mod_first", [P, 2 * KC, S], where=first)
        h_hi = sb("h_hi", [P, KC, S], f32r)
        h_lo = sb("h_lo", [P, KC, S], f32r)

        with ExitStack() as attn:
            kf = sb("kf", [HD, KV, PAD + S], f32, attn)
            vt = sb("vt", [P, PAD + S], f32, attn)
            v_s = sb("v_s", [P, NCH, P], f32, attn)
            with ExitStack() as rope:
                cos = sb("cos", [P, S], f32, rope)
                sin = sb("sin", [P, S], f32, rope)
                qa = sb("qa", [P, 2, S], f32, rope)
                qb = sb("qb", [P, 2, S], f32, rope)
                oa = sb("oa", [P, 2, S], f32, rope)
                ob = sb("ob", [P, 2, S], f32, rope)
            qf = sb("qf", [HD, 2, HALF], f32, attn)
            pr = sb("pr", [P, 2, 4, P + 1], f32, attn)
            pt = sb("pt", [P, 2, HALF], f32, attn)
            v_w = sb("v_w", [P, 2, P], f32, attn)
            small = sb("small", [P, 2, 4, 4], f32, attn)
        with ExitStack() as late:
            mod_late = sb("mod_late", [P, 2 * KC, S], where=late)
        with ExitStack() as gv:
            v_out = sb("v_out", [P, 2, S], f32, gv)
            v_stat = sb("v_stat", [P, KC, VCH, 6], f32, gv)
        hid_hi = sb("hid_hi", [P, KC, S], f32r)
        hid_lo = sb("hid_lo", [P, KC, S], f32r)

        with ExitStack() as gu:
            ws = sb("ws", [P, 4, P], f32, gu)
            bias = sb("bias", [P, 4, P], f32, gu)
            vf = sb("vf", [P, 2, KC, P], f32, gu)
            u_t = sb("u_t", [P, S], f32, gu)
        mod_acc = sb("mod_acc", [P, S])
        tmp = sb("tmp", [P, 2, S])
        mod_t = sb("mod_t", [P, 2, S])
        sumsq = mod_t[:, 1, :]

        pp = [ctx.enter_context(nc.psum_tensor(f"pp{i}", [P, S], f32)) for i in range(4)]

        ngain = lambda n: colt[:, KC * n:KC * n + KC]
        mod_b = lambda part: colt[:, 4 * KC + KC * part:4 * KC + KC * part + KC]
        o = 4 * KC + PARTS * KC
        qgain_a, qgain_b, kgain = (colt[:, o + i:o + i + 1] for i in range(3))
        inv_freq = colt[:, o + 3:o + 4]
        eps = colt[:, o + 4:o + 5]
        vgain0 = o + 5
        sink0 = vgain0 + VCH
        sel_q = colt[:, sink0 + 8:sink0 + 12]
        sel_k = colt[:, sink0 + 12:sink0 + 14]

        raw_in = [sem("raw_in0"), sem("raw_in1")]
        hi_done, lo_done = sem("hi_done"), sem("lo_done")
        gemm = sem("gemm")
        evac = [sem("evac0"), sem("evac1")]
        c_ld, const_in = sem("c_ld"), sem("const_in")
        x_ld = [sem(f"x_ld{i}") for i in range(4)]
        mf_in = [sem(f"mf_in{i}") for i in range(2 * KC)]
        pos_s = sem("pos_s")
        dv = sem("dv")
        cexp, angle, trig = sem("cexp"), sem("angle"), sem("trig")
        mt_in = [sem("mt_in0"), sem("mt_in1")]
        mt_used = sem("mt_used")
        mf_used = sem("mf_used")
        mod_mm, mod_done = sem("mod_mm"), sem("mod_done")
        sq_done, ss_done = sem("sq_done"), sem("ss_done")
        half_mm, xa_done = sem("half_mm"), sem("xa_done")
        sqa_done, ssa_done = sem("sqa_done"), sem("ssa_done")
        ss_mm, sd_done, rs_done = sem("ss_mm"), sem("sd_done"), sem("rs_done")
        rb_done, bc_done = sem("rb_done"), sem("bc_done")
        t_done, nh_done, h_done = sem("t_done"), sem("nh_done"), sem("h_done")
        q_sq, q_sum, q_ss, q_sd = sem("q_sq"), sem("q_sum"), sem("q_ss"), sem("q_sd")
        q_rc, q_rb, q_bc, q_cs = sem("q_rc"), sem("q_rb"), sem("q_bc"), sem("q_cs")
        k_normed, k_swap, k_roped, kf_in = sem("k_normed"), sem("k_swap"), sem("k_roped"), sem("kf_in")
        q_roped, q_out = sem("q_roped"), sem("q_out")
        pads = sem("pads")
        v_tr, v_cp = sem("v_tr"), sem("v_cp")
        qf_in = [sem("qf_in0"), sem("qf_in1")]
        sc_mm, p_sub, p_exp, p_sum, p_norm = sem("sc_mm"), sem("p_sub"), sem("p_exp"), sem("p_sum"), sem("p_norm")
        p_tr, p_cp, vw, pv_mm, o_hi, o_lo = (sem(n) for n in ("p_tr", "p_cp", "vw", "pv_mm", "o_hi", "o_lo"))
        p_tot, p_max = sem("p_tot"), sem("p_max")
        relu, hd_hi, hid = sem("relu"), sem("hd_hi"), sem("hid")
        vtr_mm, v_stats, v_copied = sem("vtr_mm"), sem("v_stats"), sem("v_copied")
        v_saved = [sem("v_saved0"), sem("v_saved1")]
        v_sd, v_sc, v_aggr, s_gain, ss_zero = sem("v_sd"), sem("v_sc"), sem("v_aggr"), sem("s_gain"), sem("ss_zero")
        vf_in, vn = [sem("vf_in0"), sem("vf_in1")], sem("vn")
        ws_ld, wsz = sem("ws_ld"), sem("wsz")
        sp_mm, t_mul, t_hi = sem("sp_mm"), sem("t_mul"), sem("t_hi")
        late_in = [sem("late_in0"), sem("late_in1")]
        acc_zero = sem("acc_zero")
        sink8_done = sem("sink8_done")
        saved = sem("saved")

        X_WO, X_MLP, X_G = 0, [KC, 7 * KC], 5 * KC
        HID_MLP = [2, 2 + KC * MLP_GROUPS + VCH]
        HID_G = 2 + KC * MLP_GROUPS
        RING_MLP, RING_GV = 2 * KC, 2 * KC + KC * MLP_GROUPS

        def static(*v):
            return all(isinstance(i, int) for i in v)

        def split_count(n, half, k):
            return KC + 2 * KC * (n - 1) + KC * half + k + 1

        def squares(n):
            return (KC, 2 * KC, (2 + MLP_GROUPS) * KC, (4 + MLP_GROUPS) * KC)[n]

        def columns_of(half):
            return slice(HALF * half, HALF * half + HALF)

        block = ctx.enter_context(nc.Block())

        @block.sync
        def _(sp):
            sp.dma_start(cond[:, 0, :], c_in).then_inc(c_ld, 16)
            sp.dma_start(colt[:, :], cols).then_inc(const_in, 16)
            sp.dma_start(ones[:, :], mats[:, 1, :]).then_inc(const_in, 16)
            sp.dma_start(ident[:, :], mats[:, 0, :]).then_inc(const_in, 16)
            sp.dma_start(qa[:, 0, :].bitcast(i32), pos_in).then_inc(pos_s, 16)
            for i in range(4):
                sp.dma_start(x[:, 2 * i:2 * i + 2, :], x_in[:, 2 * i:2 * i + 2, :]).then_inc(x_ld[i], 16)
            for q in range(2 * KC):
                if q == KC:
                    for s in range(2):
                        sp.dma_start(w_raw[:, s, :, :], weights[s]).then_inc(raw_in[s], 16)
                sp.dma_start(mod_first[:, q, :], mod_w[q]).then_inc(mf_in[q], 16)

            def load_block(pair, s):
                sp.wait_ge(lo_done, pair * 2 + (s - 1))
                sp.dma_start(w_raw[:, s, :, :], weights[pair * 2 + s]).then_inc(raw_in[s], 16)

            def save_q(j):
                sp.wait_ge(q_roped, j + 1)
                for i in range(4):
                    head = 4 * (j % 2) + i
                    for part, src in ((0, oa), (1, ob)):
                        sp.dma_start(q_dram[:, j // 2, 32 * part:32 * part + 32, head, :].rearrange("n d t -> d n t"),
                                     src[32 * i:32 * i + 32, j % 2, :].rearrange("d (n t) -> d n t", t=CHUNK)).then_inc(q_out, 16)

            with sp.Fori(1, 3) as pair:
                for s in range(2):
                    load_block(pair, s)
            for j in range(3):
                save_q(j)
                for s in range(2):
                    load_block(3 + j, s)
            load_block(6, 0)
            save_q(3)
            load_block(6, 1)

            def load_q(t, n, g):
                if not static(t) or t >= 2:
                    sp.wait_ge(sc_mm, t - 1)
                sp.dma_start(qf[:, g, :], q_dram[n, g]).then_inc(qf_in[g], 16)

            sp.wait_ge(q_out, 16 * 8 * 4)
            sp.wait_ge(k_roped, 2)
            for g in range(KV):
                load_q(g, 0, g)
            with sp.Fori(1, NCH) as n:
                for g in range(KV):
                    load_q(n * 2 + g, n, g)

            with sp.Fori(7, UNITS // 2) as pair:
                for s in range(2):
                    load_block(pair, s)

            for n in range(KC):
                sp.wait_ge(evac[n % 2], (UNITS - KC + n) // 2 + 1)
                sp.dma_start(out[n], x[:, n, :]).then_inc(saved, 16)
            sp.wait_ge(saved, 16 * KC)

        @block.gpsimd
        def _(pool):
            def split_lo(pair, s):
                pool.wait_ge(hi_done, pair * 2 + (s + 1))
                nc.gpsimd.tensor_tensor(out=w_lo[:, s, :, :], in0=w_raw[:, s, :, :],
                                        in1=w_hi[:, s, :, :].bitcast(f32), op=ALU.subtract).then_inc(lo_done, 1)

            nc.gpsimd.memset(kf[:, :, 0:PAD], 0.0).then_inc(pads, 1)
            nc.gpsimd.memset(vt[:, 0:PAD], 0.0).then_inc(pads, 1)
            pool.wait_ge(pads, 2)
            with pool.Fori(0, U_WO // 2 + 1) as pair:
                for s in range(2):
                    split_lo(pair, s)

            def normalise(t, g):
                pool.wait_ge(p_sum, t + 1)
                nc.gpsimd.tensor_tensor(out=pr[:, g, :, 0:P], in0=pr[:, g, :, 0:P],
                                        in1=small[:, g, 3, :].unsqueeze(2).to_broadcast([P, 4, P]),
                                        op=ALU.mult).then_inc(p_norm, 1)

            with pool.Fori(0, NCH) as n:
                for g in range(KV):
                    normalise(n * 2 + g, g)

            with pool.Fori(U_WO // 2 + 1, UNITS // 2) as pair:
                for s in range(2):
                    split_lo(pair, s)

        @block.scalar
        def _(act):
            def split_hi(pair, s):
                act.wait_ge(raw_in[s], pair * 16 + 16)
                if not static(pair) or pair:
                    act.wait_ge(gemm, pair * 2 + (s - 1))
                nc.scalar.activation(w_hi[:, s, :, :], w_raw[:, s, :, :], ACT.Copy).then_inc(hi_done, 1)

            def load_mod(q, slot):
                if not static(q) or q >= 2:
                    act.wait_ge(mt_used, q - 1)
                late = 0 if static(q) and q < RING_MLP else 2 * KC
                act.dma_start(mod_t[:, slot, :], mod_w[q + (2 * KC + late)]).then_inc(mt_in[slot], 16)

            def square(k, s):
                nc.scalar.activation(tmp[:, s, :], x[:, bass.ds(k, 1), :].rearrange("p a s -> p (a s)"),
                                     ACT.Square).then_inc(sq_done, 1)

            def deviations(n, half):
                act.wait_ge(ss_mm, 2 * n + half + 1)
                nc.scalar.activation(root[:, 4 * half:4 * half + 4], pp[2][:, HALF * half:HALF * half + 4], ACT.Sqrt,
                                     bias=eps, scale=1.0 / D).then_inc(sd_done, 1)

            def norm(n):
                act.wait_ge(mod_done, 3 * n + 2)
                with act.Fori(0, KC // 2) as i:
                    for s in range(2):
                        act.wait_ge(t_done, i * 2 + (KC * n + s + 1))
                        nc.scalar.activation(h_hi[:, bass.ds(i * 2 + s, 1), :].rearrange("p a s -> p (a s)"), tmp[:, s, :],
                                             ACT.Identity, bias=mod[:, 3 * n, bass.ds(i * 2 + s, 1)]).then_inc(nh_done, 1)

            def closing(pair, n):
                def square_half(s, half):
                    act.wait_ge(*((evac[s], pair + 1) if half else (xa_done, 2 * n - 1 + s)))
                    nc.scalar.activation(tmp[:, s, columns_of(half)], x[:, KC - 2 + s, columns_of(half)],
                                         ACT.Square).then_inc(sq_done if half else sqa_done, 1)

                def high(k, s, half):
                    act.wait_ge(t_done, k + split_count(n, half, 0))
                    nc.scalar.activation(h_hi[:, bass.ds(k, 1), columns_of(half)].rearrange("p a s -> p (a s)"),
                                         tmp[:, s, columns_of(half)], ACT.Identity,
                                         bias=mod[:, 3 * n, bass.ds(k, 1)]).then_inc(nh_done, 1)

                square_half(0, 0)
                square_half(1, 0)
                deviations(n, 0)
                square_half(0, 1)
                act.wait_ge(gemm, pair * 2 + 1)
                split_hi(pair + 1, 0)
                act.wait_ge(mod_done, 3 * n + 2)
                for k in range(4):
                    high(k, k % 2, 0)
                act.wait_ge(gemm, pair * 2 + 2)
                split_hi(pair + 1, 1)
                square_half(1, 1)
                for k in range(4, 6):
                    high(k, k % 2, 0)
                deviations(n, 1)
                for k in range(6, KC):
                    high(k, k % 2, 0)
                with act.Fori(0, KC // 2) as i:
                    for s in range(2):
                        high(i * 2 + s, s, 1)

            act.wait_ge(c_ld, 16)
            nc.scalar.activation(cond[:, 1, :], cond[:, 0, :], ACT.Exp, scale=-1.0).then_inc(cexp, 1)
            for k in range(KC):
                if k % 2 == 0:
                    act.wait_ge(x_ld[k // 2], 16)
                if k >= 2:
                    act.wait_ge(ss_done, k - 1)
                square(k, k % 2)
            act.wait_ge(const_in, 48)
            for half in range(2):
                deviations(0, half)
            split_hi(0, 0)
            split_hi(0, 1)
            norm(0)

            def head_roots(j, heads):
                act.wait_ge(q_ss, j + 1)
                nc.scalar.activation(root[:, 0:heads * KC], pp[2][:, 0:heads * KC], ACT.Sqrt,
                                     bias=eps, scale=1.0 / HD).then_inc(q_sd, 1)
                act.wait_ge(q_rc, j + 1)
                spread = tmp[:, 1, :].rearrange("p (b r h d) -> p b r h d", b=KC, h=heads, d=HD // 2)
                for r in range(4 // heads):
                    ins = nc.scalar.activation(spread[:, :, r, :, :],
                                               inv[:, 0:heads * KC].rearrange("p (b h) -> p b h", h=heads)
                                               .unsqueeze(3).to_broadcast([P, KC, heads, HD // 2]), ACT.Copy)
                ins.then_inc(q_rb, 1)

            load_mod(0, 0)
            load_mod(1, 1)

            for j in range(4):
                slot = j % 2
                act.wait_ge(gemm, 2 * j + 1)
                split_hi(j + 1, 0)
                if j >= 2:
                    act.wait_ge(q_roped, j - 1)
                nc.scalar.activation(qa[:, slot, :], pp[0][:, :], ACT.Copy).then_inc(evac[0], 1)
                if j:
                    load_mod(4 * j, 0)
                load_mod(4 * j + 2, 0) if j == 0 else load_mod(4 * j + 1, 1)
                act.wait_ge(gemm, 2 * j + 2)
                split_hi(j + 1, 1)
                nc.scalar.activation(qb[:, slot, :], pp[1][:, :], ACT.Copy).then_inc(evac[1], 1)
                if j:
                    act.wait_ge(q_roped, j)
                act.wait_ge(evac[0], j + 1)
                nc.scalar.activation(tmp[:, 0, :], qa[:, slot, :], ACT.Square).then_inc(q_sq, 1)
                act.wait_ge(evac[1], j + 1)
                nc.scalar.activation(tmp[:, 1, :], qb[:, slot, :], ACT.Square).then_inc(q_sq, 1)
                load_mod(4 * j + 3, 1) if j == 0 else load_mod(4 * j + 2, 0)
                if j == 0:
                    act.wait_ge(angle, 1)
                    nc.scalar.activation(cos[:, :], cos[:, :], ACT.Sin).then_inc(trig, 1)
                    nc.scalar.activation(sin[:, :], sin[:, :], ACT.Sin).then_inc(trig, 1)
                head_roots(j, 4)
                if j:
                    load_mod(4 * j + 3, 1)

            act.wait_ge(gemm, U_K + 1)
            act.wait_ge(q_roped, 3)
            nc.scalar.activation(qa[:, 0, :], pp[0][:, :], ACT.Copy).then_inc(evac[0], 1)
            act.wait_ge(q_roped, 4)
            act.wait_ge(evac[0], U_K // 2 + 1)
            nc.scalar.activation(tmp[:, 0, :], qa[:, 0, :], ACT.Square).then_inc(q_sq, 1)
            split_hi(5, 0)
            head_roots(4, KV)
            act.wait_ge(k_normed, 1)
            act.dma_start(qb[0:64, 0, :], qa[64:128, 0, :]).then_inc(k_swap, 16)
            act.dma_start(qb[64:128, 0, :], qa[0:64, 0, :]).then_inc(k_swap, 16)
            act.wait_ge(gemm, U_V + 1)
            nc.scalar.activation(vt[:, PAD:], pp[1][:, :], ACT.Copy).then_inc(evac[1], 1)
            split_hi(5, 1)
            for j in range(4):
                act.wait_ge(v_tr, j + 1)
                nc.scalar.activation(v_s[:, 4 * j:4 * j + 4, :],
                                     pp[3][:, 0:HALF].rearrange("p (n c) -> p n c", n=4), ACT.Copy).then_inc(v_cp, 1)
            act.wait_ge(k_roped, 2)
            for g in range(KV):
                for part in range(2):
                    act.dma_start(kf[32 * part:32 * part + 32, g, PAD:],
                                  oa[64 * part + 32 * g:64 * part + 32 * g + 32, 0, :]).then_inc(kf_in, 16)

            def probs_copy(t, g):
                act.wait_ge(p_tr, t + 1)
                if not static(t) or t >= 2:
                    act.wait_ge(pv_mm, t - 1)
                nc.scalar.activation(pt[:, g, :], pp[1][:, HALF * g:HALF * g + HALF], ACT.Copy).then_inc(p_cp, 1)

            def out_high(t, n, g):
                act.wait_ge(pv_mm, t + 1)
                rows = slice(64 * g, 64 * g + 64)
                nc.scalar.activation(h_hi[rows, :, bass.ds(n * CHUNK, CHUNK)],
                                     pp[2][rows, HALF * g:HALF * g + HALF].rearrange("p (h t) -> p h t", t=CHUNK),
                                     ACT.Copy).then_inc(o_hi, 1)

            def exps(t, g):
                act.wait_ge(p_sub, t + 1)
                nc.scalar.activation(pr[:, g, :, :], pr[:, g, :, :], ACT.Exp, scale=HD ** -0.5).then_inc(p_exp, 1)

            def window(t, n, e):
                if not static(t) or t >= 4:
                    act.wait_ge(pv_mm, t - 2)
                nc.scalar.activation(v_w[:, e, :], v_s[:, bass.ds(n, 1), :].rearrange("p a c -> p (a c)"),
                                     ACT.Copy).then_inc(vw, 1)

            def step(m, b):
                t = m * 4 + b
                if not static(t) or 2 <= t < 2 * NCH + 2:
                    probs_copy(t - 2, b % 2)
                if not static(t) or 3 <= t:
                    out_high(t - 3, m * 2 + ((b + 1) // 2 - 2), (b + 1) % 2)
                if not static(t) or t < 2 * NCH:
                    exps(t, b % 2)
                    if b % 2 == 0:
                        window(t, m * 2 + b // 2, b // 2)

            act.wait_ge(v_cp, 4)
            for b in range(4):
                step(0, b)
            with act.Fori(1, NCH // 2 - 1) as m:
                for b in range(4):
                    step(m, b)
            for b in range(7):
                step(NCH // 2 - 1 + b // 4, b % 4)

            def residual(pair0, first=0, count=4, split=True):
                with act.Fori(first, first + count) as i:
                    for s in range(2):
                        if split:
                            act.wait_ge(gemm, (i + pair0) * 2 + (s + 1))
                            split_hi(i + (pair0 + 1), s)
                        act.wait_ge(evac[s], i + (pair0 + 1))
                        square(i * 2 + s, s)

            act.wait_ge(o_lo, 2 * NCH)
            for part in range(2):
                act.dma_start(mod_late[:, KC * part:KC * part + KC, :],
                              mod_w[4 * KC + KC * part:4 * KC + KC * part + KC].rearrange("q p s -> p q s")).then_inc(late_in[part], 16)
            residual(U_WO // 2, count=3)
            closing(U_WO // 2 + 3, 1)

            def mlp(layer):
                pair0 = U_MLP[layer] // 2
                c0 = KC * MLP_GROUPS * layer

                def group(g, last=False):
                    with act.Fori(0, 4) as i:
                        for s in range(2):
                            c = g * KC + i * 2 + s
                            pair = g * 8 + i + pair0
                            if layer == 0:
                                act.wait_ge(ss_done, g * KC + 2 * KC)
                                load_mod(c + RING_MLP, s)
                            act.wait_ge(gemm, pair * 2 + (s + 1))
                            act.wait_ge(hid, c + (HID_MLP[layer] - 1))
                            nc.scalar.activation(tmp[:, s, :], pp[s][:, :], ACT.Relu).then_inc(relu, 1)
                            split_hi(pair + 1, s)
                            act.wait_ge(evac[s], pair + 1)
                            nc.scalar.activation(hid_hi[:, bass.ds(i * 2 + s, 1), :].rearrange("p a s -> p (a s)"),
                                                 tmp[:, s, :], ACT.Copy).then_inc(hd_hi, 1)
                    if last:
                        residual(g * 8 + (pair0 + 4), 0, 3)
                        if layer:
                            residual(g * 8 + (pair0 + 4), 3, 1, split=False)
                        else:
                            closing(g * 8 + (pair0 + 7), 2)
                    else:
                        residual(g * 8 + (pair0 + 4))

                with act.Fori(0, MLP_GROUPS - 1) as g:
                    group(g)
                group(MLP_GROUPS - 1, last=True)

            mlp(0)

            def v_unit(i, s):
                c = i * 2 + s
                load_mod(c + RING_GV, s)
                act.wait_ge(gemm, c + (U_GV + 1))
                split_hi(i + (U_GV // 2 + 1), s)
                if not static(c) or c >= 2:
                    act.wait_ge(vtr_mm, c - 1)
                nc.scalar.activation(tmp[:, s, :], pp[s][:, :], ACT.Gelu).then_inc(evac[s], 1)

            def v_copy(c, s, before):
                act.wait_ge(v_stats, c + 1)
                if not static(before) or before:
                    act.wait_ge(v_saved[s], before * 16)
                nc.scalar.activation(v_out[:, s, :], pp[2][:, :], ACT.Copy).then_inc(v_copied, 1)
                act.wait_ge(v_copied, c + 1)
                act.dma_start(v_dram[c], v_out[:, s, :]).then_inc(v_saved[s], 16)

            v_unit(0, 0)
            v_unit(0, 1)
            v_copy(0, 0, 0)
            v_unit(1, 0)
            v_copy(1, 1, 0)
            v_unit(1, 1)
            v_copy(2, 0, 1)
            with act.Fori(2, VCH // 2) as i:
                v_unit(i, 0)
                v_copy(i * 2 - 1, 1, i - 1)
                v_unit(i, 1)
                v_copy(i * 2, 0, i)
            v_copy(VCH - 1, 1, VCH // 2 - 1)
            act.wait_ge(v_aggr, 1)
            nc.scalar.activation(vscale[:, 0, :], vmean[:, :, 1], ACT.Sqrt, bias=eps).then_inc(v_sd, 1)
            for s in range(2):
                act.wait_ge(v_saved[s], 16 * (VCH // 2))

            act.wait_ge(wsz, 1)
            for kb in range(2):
                act.wait_ge(ss_done, kb * KC + (2 + MLP_GROUPS) * KC)
                groups = bass.ds(kb * 4, 4)
                act.dma_start(ws[0:64, :, :], ws_in[groups, 0:64, :].rearrange("g j i -> j g i")).then_inc(ws_ld, 16)
                act.dma_start(ws[64:128, :, 64:128],
                              ws_in[groups, 64:128, 64:128].rearrange("g j i -> j g i")).then_inc(ws_ld, 16)
                act.dma_start(bias[:, :, :], bias_in[groups].rearrange("g p i -> p g i")).then_inc(ws_ld, 16)
                with act.Fori(0, 4) as i:
                    for s in range(2):
                        c = kb * KC + i * 2 + s
                        pair = kb * KC + i + U_GU // 2
                        act.wait_ge(hid, c + (HID_G - 1))
                        act.dma_start(vf[:, s, :, :], v_dram[c].rearrange("p (b f) -> p b f", b=KC)).then_inc(vf_in[s], 16)
                        act.wait_ge(gemm, pair * 2 + (s + 1))
                        split_hi(pair + 1, s)
                        act.wait_ge(hid, c + HID_G)
                        nc.scalar.activation(u_t[:, :], pp[s][:, :], ACT.Gelu).then_inc(evac[s], 1)
                        act.wait_ge(t_mul, c + 1)
                        nc.scalar.activation(hid_hi[:, bass.ds(i * 2 + s, 1), :].rearrange("p a s -> p (a s)"),
                                             pp[2][:, :], ACT.Copy).then_inc(t_hi, 1)
                residual(kb * KC + (U_GU // 2 + 4), count=4 - kb)
            closing(KC + U_GU // 2 + 7, 3)
            mlp(1)

        @block.vector
        def _(dve):
            chain = [0]

            def own(ins):
                chain[0] += 1
                ins.then_inc(dv, 1)
                dve.wait_ge(dv, chain[0])

            V = nc.vector

            def add_square(idx, s, first=False):
                dve.wait_ge(sq_done, idx + 1)
                dve.wait_ge(ss_done, idx) if not static(idx) or idx else None
                V.tensor_tensor(out=sumsq, in0=sumsq, in1=tmp[:, s, :], op=ALU.add).then_inc(ss_done, 1)

            def scale_add(tile, k, counter):
                V.scalar_tensor_tensor(out=mod_acc[:, :], in0=tile, scalar=cond[:, 2, bass.ds(k, 1)],
                                       in1=mod_acc[:, :], op0=ALU.mult, op1=ALU.add).then_inc(counter, 1)

            def mod_step(q, k, slot, loads):
                dve.wait_ge(mt_in[slot], loads * 16)
                if not static(q) or q:
                    dve.wait_ge(mt_used, q)
                scale_add(mod_t[:, slot, :], k, mt_used)

            def mod_part(part):
                dve.wait_ge(mod_mm, part + 1)
                V.tensor_tensor(out=mod[:, bass.ds(part, 1), :].rearrange("p a k -> p (a k)"),
                                in0=pp[3][:, HALF:HALF + KC], in1=colt[:, bass.ds(part * KC + 4 * KC, KC)],
                                op=ALU.add).then_inc(mod_done, 1)
                V.memset(mod_acc[:, :], 0.0).then_inc(acc_zero, 1)
                dve.wait_ge(acc_zero, part)

            def deviations(n, half):
                dve.wait_ge(sd_done, 2 * n + half + 1)
                own(V.reciprocal(inv[:, 4 * half:4 * half + 4], root[:, 4 * half:4 * half + 4]))
                V.tensor_tensor(out=mod_t[:, 0, columns_of(half)].rearrange("p (b m) -> p b m", m=P),
                                in0=ident[:, :].unsqueeze(1).to_broadcast([P, 4, P]),
                                in1=inv[:, 4 * half:4 * half + 4].unsqueeze(2).to_broadcast([P, 4, P]),
                                op=ALU.mult).then_inc(rb_done, 1)

            def gains(n):
                dve.wait_ge(mod_done, 3 * n + 2)
                own(V.scalar_tensor_tensor(out=amp[:, n, :], in0=mod[:, 3 * n + 1, :], scalar=1.0,
                                           in1=ngain(n), op0=ALU.add, op1=ALU.mult))

            def norm(n):
                gains(n)
                dve.wait_ge(bc_done, 2)

                def scaled(k, s):
                    if not static(k) or k >= 2:
                        dve.wait_ge(h_done, k + (KC * n - 1))
                    V.scalar_tensor_tensor(out=tmp[:, s, :], in0=x[:, bass.ds(k, 1), :].rearrange("p a s -> p (a s)"),
                                           scalar=amp[:, n, bass.ds(k, 1)], in1=pp[2][:, :],
                                           op0=ALU.mult, op1=ALU.mult).then_inc(t_done, 1)

                def low(k, s):
                    dve.wait_ge(nh_done, k + (KC * n + 1))
                    V.scalar_tensor_tensor(out=h_lo[:, bass.ds(k, 1), :].rearrange("p a s -> p (a s)"),
                                           in0=tmp[:, s, :], scalar=mod[:, 3 * n, bass.ds(k, 1)],
                                           in1=h_hi[:, bass.ds(k, 1), :].rearrange("p a s -> p (a s)").bitcast(f32),
                                           op0=ALU.add, op1=ALU.subtract).then_inc(h_done, 1)

                scaled(0, 0)
                scaled(1, 1)
                with dve.Fori(0, KC // 2 - 1) as i:
                    for s in range(2):
                        low(i * 2 + s, s)
                        scaled(i * 2 + (s + 2), s)
                low(KC - 2, 0)
                low(KC - 1, 1)

            def closing(pair, n, gate):
                def residual_half(s, half):
                    dve.wait_ge(*((gemm, pair * 2 + s + 1) if half else (half_mm, 2 * n - 1 + s)))
                    xn = x[:, KC - 2 + s, columns_of(half)]
                    V.scalar_tensor_tensor(out=xn, in0=pp[s][:, columns_of(half)], scalar=mod[:, gate, KC - 2 + s:KC - 1 + s],
                                           in1=xn, op0=ALU.mult, op1=ALU.add).then_inc(evac[s] if half else xa_done, 1)

                def add_half(s, half):
                    before = squares(n) - 2
                    dve.wait_ge(*((sq_done, before + s + 1) if half else (sqa_done, 2 * n - 1 + s)))
                    dve.wait_ge(*((ssa_done, 2 * n - 1) if s and not half else (ss_done, before + s * half)))
                    V.tensor_tensor(out=sumsq[:, columns_of(half)], in0=sumsq[:, columns_of(half)],
                                    in1=tmp[:, s, columns_of(half)], op=ALU.add).then_inc(ss_done if half else ssa_done, 1)

                def scaled(k, s, half):
                    if not static(k) or k >= 2:
                        dve.wait_ge(h_done, k + (split_count(n, half, 0) - 2))
                    V.scalar_tensor_tensor(out=tmp[:, s, columns_of(half)],
                                           in0=x[:, bass.ds(k, 1), columns_of(half)].rearrange("p a s -> p (a s)"),
                                           scalar=amp[:, n, bass.ds(k, 1)], in1=pp[2][:, columns_of(half)],
                                           op0=ALU.mult, op1=ALU.mult).then_inc(t_done, 1)

                def low(k, s, half):
                    dve.wait_ge(nh_done, k + split_count(n, half, 0))
                    h_k = h_hi[:, bass.ds(k, 1), columns_of(half)].rearrange("p a s -> p (a s)")
                    V.scalar_tensor_tensor(out=h_lo[:, bass.ds(k, 1), columns_of(half)].rearrange("p a s -> p (a s)"),
                                           in0=tmp[:, s, columns_of(half)], scalar=mod[:, 3 * n, bass.ds(k, 1)],
                                           in1=h_k.bitcast(f32), op0=ALU.add, op1=ALU.subtract).then_inc(h_done, 1)

                residual_half(0, 0)
                residual_half(1, 0)
                add_half(0, 0)
                add_half(1, 0)
                gains(n)
                deviations(n, 0)
                residual_half(0, 1)
                dve.wait_ge(bc_done, 2 * n + 1)
                scaled(0, 0, 0)
                scaled(1, 1, 0)
                between = {1: (lambda: residual_half(1, 1),), 2: (lambda: add_half(0, 1), lambda: add_half(1, 1)),
                           3: (lambda: deviations(n, 1),)}
                for k in range(KC):
                    low(k, k % 2, 0)
                    if k + 2 < KC:
                        scaled(k + 2, k % 2, 0)
                    for step in between.get(k, ()):
                        step()
                dve.wait_ge(bc_done, 2 * n + 2)
                scaled(0, 0, 1)
                scaled(1, 1, 1)
                with dve.Fori(0, KC // 2 - 1) as i:
                    for s in range(2):
                        low(i * 2 + s, s, 1)
                        scaled(i * 2 + (s + 2), s, 1)
                low(KC - 2, 0, 1)
                low(KC - 1, 1, 1)

            V.memset(vscale[:, 0, :], 0.0).then_inc(hid, 1)
            V.memset(vscale[:, 1, :], 0.0).then_inc(hid, 1)
            own(V.memset(sumsq, 0.0))
            dve.wait_ge(cexp, 1)
            own(V.tensor_scalar(cond[:, 1, :], cond[:, 1, :], 1.0, None, ALU.add))
            own(V.reciprocal(cond[:, 1, :], cond[:, 1, :]))
            own(V.tensor_tensor(out=cond[:, 2, :], in0=cond[:, 0, :], in1=cond[:, 1, :], op=ALU.mult))
            dve.wait_ge(const_in, 48)
            V.tensor_scalar(sink8[:, :], colt[:, sink0:sink0 + 2 * 4], 8.0, None, ALU.mult).then_inc(sink8_done, 1)
            dve.wait_ge(pos_s, 16)
            own(V.tensor_copy(cos[:, :], qa[:, 0, :].bitcast(i32)))
            for k in range(KC):
                add_square(k, k % 2)
            for part in range(2):
                acc = mod_acc[:, :] if part == 0 else tmp[:, 0, :]
                for k in range(KC):
                    q = part * KC + k
                    dve.wait_ge(mf_in[q], 16)
                    if q:
                        dve.wait_ge(mf_used, q)
                    if k == 0:
                        V.tensor_scalar(acc, mod_first[:, q, :], cond[:, 2, 0:1], None, ALU.mult).then_inc(mf_used, 1)
                    else:
                        V.scalar_tensor_tensor(out=acc, in0=mod_first[:, q, :], scalar=cond[:, 2, k:k + 1],
                                               in1=acc, op0=ALU.mult, op1=ALU.add).then_inc(mf_used, 1)
                if part == 0:
                    for half in range(2):
                        deviations(0, half)
            for part in range(2):
                dve.wait_ge(mod_mm, part + 1)
                V.tensor_tensor(out=mod[:, part, :], in0=pp[3][:, HALF * (1 - part):HALF * (1 - part) + KC],
                                in1=mod_b(part), op=ALU.add).then_inc(mod_done, 1)
            norm(0)
            V.memset(mod_acc[:, :], 0.0).then_inc(acc_zero, 1)
            dve.wait_ge(acc_zero, 1)

            own(V.tensor_scalar(sin[:, :], cos[:, :], inv_freq, None, ALU.mult))
            own(V.tensor_scalar(cos[:, :], sin[:, :], 1.0 / TWO_PI, MAGIC, ALU.mult, ALU.add))
            own(V.tensor_scalar(cos[:, :], cos[:, :], MAGIC, None, ALU.subtract))
            for part in (TWO_PI_1, TWO_PI_2, TWO_PI_3):
                own(V.scalar_tensor_tensor(out=sin[:, :], in0=cos[:, :], scalar=-part, in1=sin[:, :],
                                           op0=ALU.mult, op1=ALU.add))
            own(V.tensor_scalar(sin[:, :], sin[:, :], -PI, PI, ALU.max, ALU.min))
            own(V.scalar_tensor_tensor(out=cos[:, :], in0=sin[:, :], scalar=-1.0, in1=sin[:, :],
                                       op0=ALU.mult, op1=ALU.max))
            V.tensor_scalar(cos[:, :], cos[:, :], -1.0, PI / 2, ALU.mult, ALU.add).then_inc(angle, 1)
            mod_q = [0]

            def mods(count):
                for _ in range(count):
                    q = mod_q[0]
                    mod_step(q, q % KC, q % 2, q // 2 + 1)
                    mod_q[0] += 1

            def head_reciprocals(j, heads):
                dve.wait_ge(q_sd, j + 1)
                V.reciprocal(inv[:, 0:heads * KC], root[:, 0:heads * KC]).then_inc(q_rc, 1)
                dve.wait_ge(q_bc, j + 1)

            for j in range(4):
                slot = j % 2
                if j == 2:
                    mod_part(2)
                mods(2)
                dve.wait_ge(q_sq, 2 * (j + 1))
                V.tensor_tensor(out=tmp[:, 0, :], in0=tmp[:, 0, :], in1=tmp[:, 1, :], op=ALU.add).then_inc(q_sum, 1)
                mods(1)
                head_reciprocals(j, 4)
                if j == 0:
                    dve.wait_ge(trig, 2)
                V.tensor_tensor(out=tmp[:, 0, :], in0=cos[:, :], in1=pp[2][:, :], op=ALU.mult).then_inc(q_cs, 1)
                V.tensor_tensor(out=tmp[:, 1, :], in0=sin[:, :], in1=pp[2][:, :], op=ALU.mult).then_inc(q_cs, 1)
                dve.wait_ge(q_cs, 2 * j + 2)
                if j >= 2:
                    dve.wait_ge(q_out, 16 * 8 * (j - 1))

                def turn(dst, src, gain, by):
                    own(V.scalar_tensor_tensor(out=dst[:, slot, :], in0=src[:, slot, :], scalar=gain, in1=tmp[:, by, :],
                                               op0=ALU.mult, op1=ALU.mult))

                turn(oa, qa, qgain_a, 0)
                turn(ob, qb, qgain_b, 1)
                own(V.tensor_tensor(out=oa[:, slot, :], in0=oa[:, slot, :], in1=ob[:, slot, :], op=ALU.subtract))
                turn(qb, qb, qgain_b, 0)
                turn(qa, qa, qgain_a, 1)
                V.tensor_tensor(out=ob[:, slot, :], in0=qb[:, slot, :], in1=qa[:, slot, :], op=ALU.add).then_inc(q_roped, 1)
                mods(1)

            head_reciprocals(4, KV)
            V.scalar_tensor_tensor(out=qa[:, 0, :], in0=qa[:, 0, :], scalar=kgain, in1=pp[2][:, :],
                                   op0=ALU.mult, op1=ALU.mult).then_inc(k_normed, 1)
            dve.wait_ge(k_normed, 1)
            own(V.tensor_tensor(out=tmp[:, 0, :], in0=qa[:, 0, :], in1=cos[:, :], op=ALU.mult))
            dve.wait_ge(q_out, 16 * 8 * 3)
            dve.wait_ge(k_swap, 32)
            own(V.tensor_tensor(out=tmp[:, 1, :], in0=qb[:, 0, :], in1=sin[:, :], op=ALU.mult))
            for r, op in ((slice(0, 64), ALU.subtract), (slice(64, 128), ALU.add)):
                V.tensor_tensor(out=oa[r, 0, :], in0=tmp[r, 0, :], in1=tmp[r, 1, :], op=op).then_inc(k_roped, 1)
            mod_part(3)

            def sums(t, g):
                dve.wait_ge(p_exp, t + 1)
                if not static(t) or t >= 2:
                    dve.wait_ge(p_norm, t - 1)
                V.tensor_reduce(out=small[:, g, 2, :], in_=pr[:, g, :, :], axis=X, op=ALU.add).then_inc(p_tot, 1)
                dve.wait_ge(p_tot, t + 1)
                V.reciprocal(small[:, g, 3, :], small[:, g, 2, :]).then_inc(p_sum, 1)

            def maxima(t, g):
                lo = PAD if static(t) and t < 2 else 0
                sc = pp[0][:, HALF * g:HALF * g + HALF].rearrange("p (r k) -> p r k", k=P)
                dve.wait_ge(sc_mm, t + 1)
                if not static(t) or t >= 2:
                    dve.wait_ge(p_tr, t - 1)
                V.tensor_reduce(out=small[:, g, 0, :], in_=sc[:, :, lo:], axis=X, op=ALU.max).then_inc(p_max, 1)
                dve.wait_ge(p_max, t * 2 + 1)
                V.tensor_tensor(out=small[:, g, 1, :], in0=small[:, g, 0, :], in1=sink8[:, 4 * g:4 * g + 4],
                                op=ALU.max).then_inc(p_max, 1)
                dve.wait_ge(p_max, t * 2 + 2)
                if lo:
                    V.memset(pr[:, g, :, 0:lo], -1.0e4)
                V.tensor_tensor(out=pr[:, g, :, P:P + 1], in0=sink8[:, 4 * g:4 * g + 4].unsqueeze(2),
                                in1=small[:, g, 1, :].unsqueeze(2), op=ALU.subtract)
                V.tensor_tensor(out=pr[:, g, :, lo:P], in0=sc[:, :, lo:],
                                in1=small[:, g, 1, :].unsqueeze(2).to_broadcast([P, 4, P - lo]),
                                op=ALU.subtract).then_inc(p_sub, 1)

            def out_low(t, n, g):
                rows = slice(64 * g, 64 * g + 64)
                cs = bass.ds(n * CHUNK, CHUNK)
                dve.wait_ge(o_hi, t + 1)
                V.tensor_tensor(out=h_lo[rows, :, cs],
                                in0=pp[2][rows, HALF * g:HALF * g + HALF].rearrange("p (h t) -> p h t", t=CHUNK),
                                in1=h_hi[rows, :, cs].bitcast(f32), op=ALU.subtract).then_inc(o_lo, 1)

            def step(m, b):
                t = m * 4 + b
                if not static(t) or 1 <= t < 2 * NCH + 1:
                    sums(t - 1, (b + 1) % 2)
                if not static(t) or t < 2 * NCH:
                    maxima(t, b % 2)
                if not static(t) or 3 <= t:
                    out_low(t - 3, m * 2 + ((b + 1) // 2 - 2), (b + 1) % 2)

            dve.wait_ge(sink8_done, 1)
            for b in range(4):
                step(0, b)
            with dve.Fori(1, NCH // 2 - 1) as m:
                for b in range(4):
                    step(m, b)
            for b in range(7):
                step(NCH // 2 - 1 + b // 4, b % 4)

            def residual(pair0, n0, gate, first=0, count=4, late=None, zeroed=None):
                with dve.Fori(first, first + count) as i:
                    for s in range(2):
                        if late is not None:
                            tiles = KC // (2 * count)
                            for r in range(tiles):
                                k = (i - first) * (2 * tiles) + (tiles * s + r)
                                dve.wait_ge(mf_used, k + (2 * KC + KC * late))
                                scale_add(mod_late[:, bass.ds(k + KC * late, 1), :].rearrange("p a s -> p (a s)"), k, mf_used)
                        xn = x[:, bass.ds(i * 2 + s, 1), :].rearrange("p a s -> p (a s)")
                        dve.wait_ge(gemm, (i + pair0) * 2 + (s + 1))
                        V.scalar_tensor_tensor(out=xn, in0=pp[s][:, :], scalar=mod[:, gate, bass.ds(i * 2 + s, 1)],
                                               in1=xn, op0=ALU.mult, op1=ALU.add).then_inc(evac[s], 1)
                        if zeroed is not None:
                            dve.wait_ge(ss_zero, zeroed)
                        add_square(i * 2 + (n0 + KC + s), s)

            own(V.memset(sumsq, 0.0))
            for late in range(2):
                dve.wait_ge(late_in[late], 16)
                residual(U_WO // 2, X_WO, GATE1, 2 * late, 2 - late, late)
                mod_part(4 + late)
            closing(U_WO // 2 + 3, 1, GATE1)

            def mlp(layer):
                pair0 = U_MLP[layer] // 2
                c0 = KC * MLP_GROUPS * layer
                def group(g, last=False):
                    with dve.Fori(0, 4) as i:
                        for s in range(2):
                            c = g * KC + i * 2 + s
                            if layer == 0:
                                mod_step(c + RING_MLP, i * 2 + s, s, g * 4 + i + (RING_MLP // 2 + 1))
                            dve.wait_ge(relu, c + (c0 + 1))
                            V.scalar_tensor_tensor(out=tmp[:, s, :], in0=pp[s][:, :], scalar=0.0, in1=tmp[:, s, :],
                                                   op0=ALU.max, op1=ALU.mult).then_inc(evac[s], 1)
                            dve.wait_ge(hd_hi, c + (c0 + 1))
                            V.tensor_tensor(out=hid_lo[:, bass.ds(i * 2 + s, 1), :].rearrange("p a s -> p (a s)"),
                                            in0=tmp[:, s, :],
                                            in1=hid_hi[:, bass.ds(i * 2 + s, 1), :].rearrange("p a s -> p (a s)").bitcast(f32),
                                            op=ALU.subtract).then_inc(hid, 1)
                    if layer == 0:
                        mod_part(g + 6)
                    V.memset(sumsq, 0.0).then_inc(ss_zero, 1)
                    close = last and layer == 0
                    residual(g * 8 + (pair0 + 4), g * KC + X_MLP[layer], 6 * layer + GATE2, count=3 if close else 4,
                             zeroed=g + (1 + layer * (MLP_GROUPS + 2)))
                    if close:
                        closing(g * 8 + (pair0 + 7), 2, GATE2)

                with dve.Fori(0, MLP_GROUPS - 1) as g:
                    group(g)
                group(MLP_GROUPS - 1, last=True)

            mlp(0)

            for half in range(2):
                with dve.Fori(4 * half, 4 * half + 4) as i:
                    for s in range(2):
                        c = i * 2 + s
                        mod_step(c + RING_GV, c - KC * half, s, i + (RING_GV // 2 + 1))
                        dve.wait_ge(vtr_mm, c + 1)
                        for b in range(KC):
                            ins = V.bn_stats(v_stat[:, b, bass.ds(c, 1), :].rearrange("p a s -> p (a s)"),
                                             pp[2][:, P * b:P * b + P])
                        ins.then_inc(v_stats, 1)
                mod_part(10 + half)
            dve.wait_ge(v_stats, VCH)
            for b in range(KC):
                ins = V.bn_aggr(vmean[:, b, :], v_stat[:, b, :, :].rearrange("p c s -> p (c s)"))
            ins.then_inc(v_aggr, 1)
            dve.wait_ge(v_sd, 1)
            own(V.reciprocal(vscale[:, 0, :], vscale[:, 0, :]))
            V.scalar_tensor_tensor(out=vscale[:, 1, :], in0=vmean[:, :, 0], scalar=-1.0, in1=vscale[:, 0, :],
                                   op0=ALU.mult, op1=ALU.mult).then_inc(v_sc, 1)
            dve.wait_ge(v_sc, 1)
            V.memset(ws[64:128, :, 0:64], 0.0).then_inc(wsz, 1)

            for kb in range(2):
                with dve.Fori(0, 4) as i:
                    for s in range(2):
                        c = kb * KC + i * 2 + s
                        pair = kb * KC + i + U_GU // 2
                        dve.wait_ge(vf_in[s], kb * 64 + i * 16 + 16)
                        for b in range(KC):
                            ins = V.tensor_scalar(vf[:, s, b, :], vf[:, s, b, :], vscale[:, 0, b:b + 1],
                                                  vscale[:, 1, b:b + 1], ALU.mult, ALU.add)
                        ins.then_inc(vn, 1)
                        mixed = pp[2][:, :].rearrange("p (b t) -> p b t", b=KC)
                        dve.wait_ge(sp_mm, c + 1)
                        V.scalar_tensor_tensor(out=mixed, in0=mixed, scalar=colt[:, bass.ds(c + vgain0, 1)],
                                               in1=bias[:, bass.ds(i, 1), :].to_broadcast([P, KC, P]),
                                               op0=ALU.mult, op1=ALU.add).then_inc(s_gain, 1)
                        dve.wait_ge(s_gain, c + 1)
                        dve.wait_ge(evac[s], pair + 1)
                        V.tensor_tensor(out=pp[2][:, :], in0=pp[2][:, :], in1=u_t[:, :], op=ALU.mult).then_inc(t_mul, 1)
                        dve.wait_ge(t_hi, c + 1)
                        V.tensor_tensor(out=hid_lo[:, bass.ds(i * 2 + s, 1), :].rearrange("p a s -> p (a s)"),
                                        in0=pp[2][:, :],
                                        in1=hid_hi[:, bass.ds(i * 2 + s, 1), :].rearrange("p a s -> p (a s)").bitcast(f32),
                                        op=ALU.subtract).then_inc(hid, 1)
                V.memset(sumsq, 0.0).then_inc(ss_zero, 1)
                residual(kb * KC + (U_GU // 2 + 4), kb * KC + X_G, 6 + GATE1, count=4 - kb,
                         zeroed=kb + (MLP_GROUPS + 1))
            closing(KC + U_GU // 2 + 7, 3, 6 + GATE1)
            mlp(1)

        @block.tensor
        def _(pe):
            T = nc.tensor

            def ready(pair, s):
                pe.wait_ge(lo_done, pair * 2 + (s + 1))
                if not static(pair) or pair:
                    pe.wait_ge(evac[s], pair)

            def products(s, k, hi, lo, halves=(0, 1)):
                for w, parts in ((w_hi, (hi, lo)), (w_lo, (hi,))):
                    for r in parts:
                        for half in halves:
                            cs = columns_of(half)
                            last = T.matmul(pp[s][:, cs], w[:, s, k, :], r[:, k, cs],
                                            start=(k == 0 and w is w_hi and r is hi),
                                            stop=(k == KC - 1 and w is w_lo))
                return last

            def unit(pair, s, hi, lo, chunk_ready=None, hooks=None):
                ready(pair, s)
                for k in range(KC):
                    if chunk_ready:
                        pe.wait_ge(chunk_ready[0], chunk_ready[1] + k)
                    last = products(s, k, hi, lo)
                    if hooks and k in hooks:
                        hooks[k]()
                last.then_inc(gemm, 1)

            def normed_pair(pair):
                ready(pair, 0)
                ready(pair, 1)
                for k in range(KC + LAG):
                    if k < KC:
                        pe.wait_ge(h_done, k + 1)
                        last = products(0, k, h_hi, h_lo)
                        if k == KC - 1:
                            last.then_inc(gemm, 1)
                    if k >= LAG:
                        last = products(1, k - LAG, h_hi, h_lo)
                last.then_inc(gemm, 1)

            def closing_pair(pair, hi, lo, n, columns=None):
                for half in range(2):
                    for s in range(2):
                        if half == 0:
                            ready(pair, s)
                        for k in range(KC):
                            last = products(s, k, hi, lo, (half,))
                            if (half, s, k) == (0, 0, 5) and columns:
                                columns()
                            if (half, s, k) == (1, 0, 4):
                                token_squares(n, 0)
                            if (half, s, k) == (1, 1, 0):
                                spread_norm(n, 0)
                        last.then_inc(gemm if half else half_mm, 1)

            def opening_pair(pair, n):
                ready(pair, 0)
                for half in range(2):
                    for k in range(KC + LAG):
                        if half == 0 and k == LAG:
                            ready(pair, 1)
                        if k < KC:
                            pe.wait_ge(h_done, split_count(n, half, k))
                            last = products(0, k, h_hi, h_lo, (half,))
                            if half and k == KC - 1:
                                last.then_inc(gemm, 1)
                        if k >= LAG:
                            last = products(1, k - LAG, h_hi, h_lo, (half,))
                        if half == 0 and k == LAG:
                            token_squares(n, 1)
                        if half == 0 and k == LAG + 2:
                            spread_norm(n, 1)
                last.then_inc(gemm, 1)

            def mod_columns(part, counter, count, acc=None, place=HALF):
                pe.wait_ge(counter, count)
                acc = mod_acc[:, :] if acc is None else acc
                for k in range(KC):
                    last = T.matmul(pp[3][:, place + k:place + k + 1], acc[:, P * k:P * k + P], ones[:, 0:1],
                                    start=True, stop=True)
                last.then_inc(mod_mm, 1)

            def token_sums(heads, select, counter):
                for b in range(KC):
                    last = T.matmul(pp[2][:, heads * b:heads * b + heads], tmp[:, 0, P * b:P * b + P], select,
                                    start=True, stop=True)
                last.then_inc(counter, 1)

            def spread(counter):
                for b in range(KC):
                    last = T.matmul(pp[2][:, P * b:P * b + P], tmp[:, 1, P * b:P * b + P], ident[:, :],
                                    start=True, stop=True)
                last.then_inc(counter, 1)

            def token_squares(n, half):
                pe.wait_ge(*((ss_done, squares(n)) if half or not n else (ssa_done, 2 * n)))
                for b in range(4):
                    last = T.matmul(pp[2][:, HALF * half + b:HALF * half + b + 1],
                                    sumsq[:, HALF * half + P * b:HALF * half + P * b + P], ones[:, 0:1],
                                    start=True, stop=True)
                last.then_inc(ss_mm, 1)

            def spread_norm(n, half):
                pe.wait_ge(rb_done, 2 * n + half + 1)
                T.matmul(pp[2][:, columns_of(half)], ones[:, :], mod_t[:, 0, columns_of(half)],
                         start=True, stop=True).then_inc(bc_done, 1)

            pe.wait_ge(const_in, 48)
            for half in range(2):
                token_squares(0, half)
            mod_columns(0, mf_used, KC)
            for half in range(2):
                spread_norm(0, half)
            mod_columns(1, mf_used, 2 * KC, tmp[:, 0, :], 0)

            def head_squares(j):
                if j == 4:
                    pe.wait_ge(q_sq, 9)
                else:
                    pe.wait_ge(q_sum, j + 1)
                if j:
                    pe.wait_ge(q_cs, 2 * j)
                token_sums(*((KV, sel_k) if j == 4 else (4, sel_q)), q_ss)

            def head_spread(j):
                pe.wait_ge(q_rb, j + 1)
                spread(q_bc)

            normed_pair(0)
            for j in range(3):
                unit(1 + j, 0, h_hi, h_lo, hooks={3: lambda: head_squares(j), 6: lambda: head_spread(j)})
                unit(1 + j, 1, h_hi, h_lo)
                if j == 1:
                    mod_columns(2, mt_used, KC)
            unit(4, 0, h_hi, h_lo, hooks={3: lambda: head_squares(3), 6: lambda: head_spread(3)})
            unit(4, 1, h_hi, h_lo, hooks={4: lambda: head_squares(4), 7: lambda: head_spread(4)})
            pe.wait_ge(evac[1], U_V // 2 + 1)
            pe.wait_ge(pads, 2)
            for j in range(4):
                if j:
                    pe.wait_ge(v_cp, j)
                for r in range(4):
                    n = 4 * j + r
                    last = T.transpose(pp[3][:, P * r:P * r + P], vt[:, CHUNK * n:CHUNK * n + P], ident[:, :])
                last.then_inc(v_tr, 1)
            mod_columns(3, mt_used, 2 * KC)

            def scores(t, n, g):
                pe.wait_ge(qf_in[g], n * 16 + 16)
                if not static(t) or t >= 2:
                    pe.wait_ge(p_sub, t - 1)
                for r in range(4):
                    last = T.matmul(pp[0][:, HALF * g + P * r:HALF * g + P * r + P], qf[:, g, P * r:P * r + P],
                                    kf[:, g, bass.ds(n * CHUNK, P)], start=True, stop=True)
                last.then_inc(sc_mm, 1)

            def turn(t, g):
                pe.wait_ge(p_norm, t + 1)
                if not static(t) or t >= 2:
                    pe.wait_ge(p_cp, t - 1)
                for r in range(4):
                    last = T.transpose(pp[1][:, HALF * g + P * r:HALF * g + P * r + P], pr[:, g, r, 0:P], ident[:, :])
                last.then_inc(p_tr, 1)

            def mix(t, n, g, e):
                pe.wait_ge(p_cp, t + 1)
                pe.wait_ge(vw, n + 1)
                if not static(t) or t >= 2:
                    pe.wait_ge(o_lo, t - 1)
                T.matmul(pp[2][:, HALF * g:HALF * g + HALF], v_w[:, e, :], pt[:, g, :],
                         start=True, stop=True).then_inc(pv_mm, 1)

            def step(m, b):
                t = m * 4 + b
                if not static(t) or t + 1 < 2 * NCH:
                    scores(t + 1, m * 2 + (b + 1) // 2, (b + 1) % 2)
                if not static(t) or 2 <= t < 2 * NCH + 2:
                    mix(t - 2, m * 2 + (b // 2 - 1), b % 2, (b // 2 + 1) % 2)
                if not static(t) or 1 <= t < 2 * NCH + 1:
                    turn(t - 1, (b + 1) % 2)

            pe.wait_ge(kf_in, 16 * 4)
            pe.wait_ge(evac[0], U_WO // 2)
            pe.wait_ge(evac[1], U_WO // 2)
            pe.wait_ge(q_cs, 8)
            scores(0, 0, 0)
            for b in range(4):
                step(0, b)
            with pe.Fori(1, NCH // 2 - 1) as m:
                for b in range(4):
                    step(m, b)
            for b in range(6):
                step(NCH // 2 - 1 + b // 4, b % 4)

            pe.wait_ge(o_lo, 2 * NCH)
            for late in range(2):
                with pe.Fori(U_WO // 2 + 2 * late, U_WO // 2 + 2 * late + 1) as pair:
                    for s in range(2):
                        unit(pair, s, h_hi, h_lo)
                if late == 0:
                    unit(U_WO // 2 + 1, 0, h_hi, h_lo)
                    unit(U_WO // 2 + 1, 1, h_hi, h_lo, hooks={5: lambda: mod_columns(4, mf_used, 3 * KC)})
            closing_pair(U_WO // 2 + 3, h_hi, h_lo, 1, lambda: mod_columns(5, mf_used, 4 * KC))

            def h_units(pair0, first, count=4):
                with pe.Fori(first, count) as i:
                    for s in range(2):
                        unit(i + pair0, s, h_hi, h_lo)

            def hid_units(pair0, hid0, after=None, close=None):
                unit(pair0, 0, hid_hi, hid_lo, (hid, hid0 + 1))
                if after:
                    after()
                unit(pair0, 1, hid_hi, hid_lo)
                with pe.Fori(1, 3 if close else 4) as i:
                    for s in range(2):
                        unit(i + pair0, s, hid_hi, hid_lo)
                if close:
                    closing_pair(pair0 + 3, hid_hi, hid_lo, close)

            def mlp(layer):
                pair0 = U_MLP[layer] // 2
                opening_pair(pair0, 2 * layer + 1)
                h_units(pair0, 1)

                def down(g, close=None):
                    columns = (lambda: mod_columns(g + 6, mt_used, g * KC + (RING_MLP + KC))) if layer == 0 else None
                    hid_units(g * 8 + (pair0 + 4), g * KC + HID_MLP[layer], columns, close)

                down(0)
                with pe.Fori(1, MLP_GROUPS - 1 + layer) as g:
                    h_units(g * 8 + pair0, 0)
                    down(g)
                if layer == 0:
                    h_units((MLP_GROUPS - 1) * 8 + pair0, 0)
                    down(MLP_GROUPS - 1, 2)

            mlp(0)

            def v_turn(c, s, pair):
                pe.wait_ge(evac[s], pair + 1)
                if not static(c) or c:
                    pe.wait_ge(v_copied, c)
                for b in range(KC):
                    last = T.transpose(pp[2][:, P * b:P * b + P], tmp[:, s, P * b:P * b + P], ident[:, :])
                last.then_inc(vtr_mm, 1)

            gv = U_GV // 2
            opening_pair(gv, 2)
            v_turn(0, 0, gv)
            with pe.Fori(1, 4) as i:
                unit(i + gv, 0, h_hi, h_lo)
                v_turn(i * 2 - 1, 1, i + (gv - 1))
                unit(i + gv, 1, h_hi, h_lo)
                v_turn(i * 2, 0, i + gv)
            unit(gv + 4, 0, h_hi, h_lo)
            v_turn(7, 1, gv + 3)
            mod_columns(10, mt_used, RING_GV + KC)
            unit(gv + 4, 1, h_hi, h_lo)
            v_turn(8, 0, gv + 4)
            with pe.Fori(5, 8) as i:
                unit(i + gv, 0, h_hi, h_lo)
                v_turn(i * 2 - 1, 1, i + (gv - 1))
                unit(i + gv, 1, h_hi, h_lo)
                v_turn(i * 2, 0, i + gv)
            v_turn(VCH - 1, 1, gv + 7)
            mod_columns(11, mt_used, RING_GV + 2 * KC)

            def blend(c, s, kb, i):
                pe.wait_ge(vn, c + 1)
                pe.wait_ge(ws_ld, kb * 48 + 48)
                pe.wait_ge(hid, c + HID_G)
                for b in range(KC):
                    last = T.matmul(pp[2][:, P * b:P * b + P], vf[:, s, b, :],
                                    ws[:, bass.ds(i, 1), :].rearrange("p a t -> p (a t)"), start=True, stop=True)
                last.then_inc(sp_mm, 1)

            for kb in range(2):
                with pe.Fori(0, 4) as i:
                    for s in range(2):
                        unit(kb * KC + i + U_GU // 2, s, h_hi, h_lo)
                        blend(kb * KC + i * 2 + s, s, kb, i)
                hid_units(kb * KC + (U_GU // 2 + 4), kb * KC + HID_G, close=3 if kb else None)
            mlp(1)


def kernel(x, c, positions, norm1_gain, norm2_gain, mod_w, mod_b, swa_w_qkv, swa_q_gain, swa_k_gain,
           swa_sinks, swa_w_o, gmlp_w_uv, gmlp_v_gain, gmlp_w_s, gmlp_s_bias, gmlp_w_o, sb_w_qkv, sb_w_o,
           mlp_w1, mlp_w2):
    import numpy as np
    import concourse.bacc as bacc
    from concourse.bass_utils import run_bass_kernel_spmd

    def blocks(w):
        k, n = w.shape
        return w.reshape(k // D, KC, P, n // P, P).transpose(0, 3, 2, 1, 4)

    def columns(v):
        return v.reshape(-1, P).T

    f = {k: np.asarray(v) for k, v in dict(
        x=x, c=c, positions=positions, n1=norm1_gain, n2=norm2_gain, mw=mod_w, mb=mod_b, qkv=swa_w_qkv, qg=swa_q_gain,
        kg=swa_k_gain, sinks=swa_sinks, wo=swa_w_o, uv=gmlp_w_uv, vg=gmlp_v_gain, ws=gmlp_w_s, sb=gmlp_s_bias,
        go=gmlp_w_o, w1=mlp_w1, w2=mlp_w2).items()}
    wq = f["qkv"][0][:, :HEADS * HD].reshape(D, 4, 4, 2, HD // 2).transpose(0, 1, 3, 2, 4).reshape(D, HEADS * HD)
    wk = f["qkv"][0][:, HEADS * HD:HEADS * HD + P].reshape(D, KV, 2, HD // 2).transpose(0, 2, 1, 3).reshape(D, P)
    wv = f["qkv"][0][:, HEADS * HD + P:]
    wo = f["wo"][0].reshape(KV, GROUP, HD, D).transpose(1, 0, 2, 3).reshape(D, D)
    order = [blocks(wq)[0], blocks(wk)[0], blocks(wv)[0], blocks(wo)[0]]

    def mlp_blocks(layer):
        up, down = blocks(f["w1"][layer])[0], blocks(f["w2"][layer])
        for g in range(MLP_GROUPS):
            order.extend((up[KC * g:KC * g + KC], down[g]))

    mlp_blocks(0)
    uv, go = blocks(f["uv"][0])[0], blocks(f["go"][0])
    order.append(uv[VCH:])
    for kb in range(2):
        order.extend((uv[KC * kb:KC * kb + KC], go[kb]))
    mlp_blocks(1)

    half = np.concatenate([f["qg"][0][:HD // 2]] * 4), np.concatenate([f["qg"][0][HD // 2:]] * 4)
    kgain = np.concatenate([f["kg"][0][:HD // 2]] * 2 + [f["kg"][0][HD // 2:]] * 2)
    freq = (10000.0 ** (-np.arange(0, HD, 2) / HD)).astype(np.float32)
    sinks = np.repeat(f["sinks"][0].reshape(KV * 4, 2).T, CHUNK, axis=0)
    cols = np.concatenate(
        [columns(g) for g in (f["n1"][0], f["n2"][0], f["n1"][1], f["n2"][1])]
        + [columns(f["mb"].reshape(-1))]
        + [a[:, None] for a in (half[0], half[1], kgain, np.tile(freq, 4), np.full(P, EPS, np.float32))]
        + [columns(f["vg"][0]), sinks, (np.arange(P)[:, None] // 32 == np.arange(4)).astype(np.float32),
           (np.arange(P)[:, None] // 32 % 2 == np.arange(KV)).astype(np.float32)], axis=1)
    mats = np.stack([np.eye(P), np.ones((P, P))], axis=1).astype(np.float32)
    arrays = {
        "x_in": f["x"][0].T.reshape(KC, P, S).transpose(1, 0, 2),
        "c_in": columns(f["c"][0]),
        "pos_in": np.broadcast_to(f["positions"][0], (P, S)),
        "weights": np.concatenate(order),
        "mod_w": f["mw"].reshape(2, KC, P, 6, D).transpose(0, 3, 1, 2, 4).reshape(PARTS * KC, P, D),
        "cols": cols,
        "mats": mats,
        "ws_in": f["ws"][0].transpose(0, 2, 1),
        "bias_in": np.broadcast_to(f["sb"][0][:, None, :], (KC, P, P)),
    }
    arrays = {k: np.ascontiguousarray(v) for k, v in arrays.items()}
    nc = bacc.Bacc("TRN2", target_bir_lowering=False, num_devices=1)
    dram = {k: nc.dram_tensor(k, a.shape, mybir.dt.from_np(a.dtype), kind="ExternalInput").ap() for k, a in arrays.items()}
    q_dram = nc.dram_tensor("q_dram", (NCH, KV, HD, GROUP, CHUNK), mybir.dt.float32, kind="Internal").ap()
    v_dram = nc.dram_tensor("v_dram", (VCH, P, S), mybir.dt.float32, kind="Internal").ap()
    out = nc.dram_tensor("out", (KC, P, S), mybir.dt.float32, kind="ExternalOutput").ap()
    build(nc, q_dram=q_dram, v_dram=v_dram, out=out, **dram)
    got = run_bass_kernel_spmd(nc, [arrays], core_ids=[0]).results[0]["out"]
    return np.ascontiguousarray(got.reshape(D, S).T)[None]
```
